# Optimizing a Trainium2 kernel written in Bass

```python
import jax, jax.numpy as jnp
from jax import lax
import numpy as np
import math
import jax
import jax.numpy as jnp

D_MODEL = 1024
BATCH = 1
SEQ = 512
DEPTH = 2

HEAD_DIM = 64
N_HEADS_TOTAL = D_MODEL // HEAD_DIM
N_HEADS_A = N_HEADS_TOTAL // 4
N_HEADS_B = N_HEADS_TOTAL // 4
N_HEADS_C = N_HEADS_TOTAL // 2
N_KV_C = N_HEADS_C // 4
N_IDX_HEADS = 4
IDX_DIM = HEAD_DIM
TOPK_MAX = 256
WINDOW = 128
BLOCK = 128
ROPE_THETA = 10000.0
NORM_EPS = 1e-6
MIX_WIDTH = N_HEADS_TOTAL * HEAD_DIM
D_FF = -(-8 * D_MODEL // (3 * 256)) * 256
_COLS = (N_HEADS_A * HEAD_DIM, HEAD_DIM, HEAD_DIM,
         N_IDX_HEADS * IDX_DIM, IDX_DIM, N_IDX_HEADS,
         N_HEADS_B * HEAD_DIM, N_HEADS_B * HEAD_DIM, N_HEADS_B * HEAD_DIM,
         N_HEADS_C * HEAD_DIM, N_KV_C * HEAD_DIM, N_KV_C * HEAD_DIM)
IN_COLS = sum(_COLS)


def _rms(x, g):
    xf = x.astype(jnp.float32)
    y = xf * lax.rsqrt(jnp.mean(xf * xf, axis=-1, keepdims=True) + NORM_EPS)
    return (y * g.astype(jnp.float32)).astype(x.dtype)

def _rope_tables(L):
    inv = 1.0 / (ROPE_THETA ** (jnp.arange(0, HEAD_DIM, 2, dtype=jnp.float32) / HEAD_DIM))
    ang = jnp.arange(L, dtype=jnp.float32)[:, None] * inv[None, :]
    return jnp.cos(ang), jnp.sin(ang)

def _rope(x, cos, sin):
    c = cos[None, :, None, :].astype(x.dtype)
    s = sin[None, :, None, :].astype(x.dtype)
    x1, x2 = jnp.split(x, 2, axis=-1)
    return jnp.concatenate([x1 * c - x2 * s, x2 * c + x1 * s], axis=-1)

def _blocks(a):
    B, L = a.shape[:2]
    return jnp.moveaxis(a.reshape((B, L // BLOCK, BLOCK) + a.shape[2:]), 1, 0)

def _unblocks(a):
    nb, B = a.shape[:2]
    return jnp.moveaxis(a, 0, 1).reshape((B, nb * BLOCK) + a.shape[3:])

def _split_points():
    pts, acc = [], 0
    for w in _COLS[:-1]:
        acc += w
        pts.append(acc)
    return pts

def _dsa(q, k, v, qi, ki, wi):
    B, L, H, D = q.shape
    n_sel = min(TOPK_MAX, L // 4)
    scale = D ** -0.5
    idx_scale = (N_IDX_HEADS * IDX_DIM) ** -0.5
    kpos = jnp.arange(L)

    def one_block(inp):
        qn, qin, win, n = inp
        tq = n * BLOCK + jnp.arange(BLOCK)
        rel = jax.nn.relu(jnp.einsum('bqhd,bsd->bqhs', qin, ki).astype(jnp.float32))
        score = jnp.einsum('bqh,bqhs->bqs', win.astype(jnp.float32), rel) * idx_scale
        causal = kpos[None, :] <= tq[:, None]
        score = jnp.where(causal[None], score, -jnp.inf)
        _, sel = lax.top_k(score, n_sel)
        valid = sel <= tq[None, :, None]
        ks = jax.vmap(lambda a, i: a[i])(k, sel)
        vs = jax.vmap(lambda a, i: a[i])(v, sel)
        s = jnp.einsum('bqhd,bqkd->bhqk', qn, ks).astype(jnp.float32) * scale
        s = jnp.where(valid[:, None], s, -jnp.inf)
        p = jax.nn.softmax(s, axis=-1)
        return jnp.einsum('bhqk,bqkd->bqhd', p.astype(vs.dtype), vs)

    out = lax.map(one_block, (_blocks(q), _blocks(qi), _blocks(wi), jnp.arange(L // BLOCK)))
    return _unblocks(out)

def _stick_breaking(q, k, v):
    B, L, H, D = q.shape
    scale = D ** -0.5
    kpos = jnp.arange(L)

    def one_block(inp):
        qn, n = inp
        tq = n * BLOCK + jnp.arange(BLOCK)
        strict = (kpos[None, :] < tq[:, None])[None, None]
        z = jnp.einsum('bqhd,bshd->bhqs', qn, k).astype(jnp.float32) * scale
        log_keep = jnp.where(strict, jax.nn.log_sigmoid(-z), 0.0)
        log_between = lax.cumsum(log_keep, axis=3, reverse=True) - log_keep
        a = jnp.where(strict, jnp.exp(jax.nn.log_sigmoid(z) + log_between), 0.0)
        return jnp.einsum('bhqs,bshd->bqhd', a.astype(v.dtype), v)

    out = lax.map(one_block, (_blocks(q), jnp.arange(L // BLOCK)))
    return _unblocks(out)

def _swa_sinks(q, k, v, sinks):
    B, L, H, D = q.shape
    G = H // N_KV_C
    nb = L // BLOCK
    scale = D ** -0.5
    pad = ((0, 0), (1, 0), (0, 0), (0, 0), (0, 0))
    kb = k.reshape(B, nb, BLOCK, N_KV_C, D)
    vb = v.reshape(B, nb, BLOCK, N_KV_C, D)
    kk = jnp.concatenate([jnp.pad(kb, pad)[:, :-1], kb], axis=2)
    vv = jnp.concatenate([jnp.pad(vb, pad)[:, :-1], vb], axis=2)
    qg = q.reshape(B, nb, BLOCK, N_KV_C, G, D)
    kloc = jnp.arange(2 * BLOCK)
    diff = (jnp.arange(BLOCK)[:, None] + BLOCK) - kloc[None, :]
    band = (diff >= 0) & (diff < WINDOW)
    sink = sinks.astype(jnp.float32).reshape(N_KV_C, G)[None, :, :, None, None]

    def one_block(inp):
        qn, kn, vn, n = inp
        s = jnp.einsum('bqkgd,bskd->bkgqs', qn, kn).astype(jnp.float32) * scale
        mask = band & ((n > 0) | (kloc >= BLOCK))[None, :]
        s = jnp.where(mask, s, -jnp.inf)
        m = jnp.maximum(jnp.max(s, axis=-1, keepdims=True), sink)
        e = jnp.exp(s - m)
        p = e / (jnp.sum(e, axis=-1, keepdims=True) + jnp.exp(sink - m))
        return jnp.einsum('bkgqs,bskd->bqkgd', p.astype(vn.dtype), vn)

    out = lax.map(one_block, (jnp.moveaxis(qg, 1, 0), jnp.moveaxis(kk, 1, 0),
                              jnp.moveaxis(vv, 1, 0), jnp.arange(nb)))
    return _unblocks(out).reshape(B, L, H, D)

def _mixing(h, w_in, qn_a, kn_a, qn_c, kn_c, sinks, g_out, w_o, cos, sin):
    B, L, _ = h.shape
    p = h @ w_in
    qa, ka, va, qi, ki, wi, qb, kb, vb, qc, kc, vc = jnp.split(p, _split_points(), axis=-1)
    qa = _rope(_rms(qa.reshape(B, L, N_HEADS_A, HEAD_DIM), qn_a), cos, sin)
    ka = _rope(_rms(ka.reshape(B, L, 1, HEAD_DIM), kn_a), cos, sin)[:, :, 0]
    qi = _rope(qi.reshape(B, L, N_IDX_HEADS, IDX_DIM), cos, sin)
    ki = _rope(ki.reshape(B, L, 1, IDX_DIM), cos, sin)[:, :, 0]
    oa = _dsa(qa, ka, va, qi, ki, wi)
    ob = _stick_breaking(qb.reshape(B, L, N_HEADS_B, HEAD_DIM),
                         kb.reshape(B, L, N_HEADS_B, HEAD_DIM),
                         vb.reshape(B, L, N_HEADS_B, HEAD_DIM))
    qc = _rope(_rms(qc.reshape(B, L, N_HEADS_C, HEAD_DIM), qn_c), cos, sin)
    kc = _rope(_rms(kc.reshape(B, L, N_KV_C, HEAD_DIM), kn_c), cos, sin)
    oc = _swa_sinks(qc, kc, vc.reshape(B, L, N_KV_C, HEAD_DIM), sinks)
    o = jnp.concatenate([oa, ob, oc], axis=2)
    o = _rms(o, g_out).reshape(B, L, MIX_WIDTH)
    return o @ w_o

def _swiglu(h, w_gate, w_up, w_down):
    return (jax.nn.silu(h @ w_gate) * (h @ w_up)) @ w_down

def first_inputs(seed: int = 0) -> dict:
    key = jax.random.key(seed)
    ks = jax.random.split(key, 20)
    f = jnp.float32
    D = D_MODEL

    def nrm(k, shape, scale):
        return jax.random.normal(k, shape, f) * scale

    def gain(k, shape):
        return 1.0 + 0.02 * jax.random.normal(k, shape, f)

    return {
        "x": nrm(ks[0], (BATCH, SEQ, D), 1.0),
        "c": nrm(ks[1], (BATCH, D), 1.0),
        "ln1": gain(ks[2], (DEPTH, D)),
        "ln2": gain(ks[3], (DEPTH, D)),
        "w_mod": nrm(ks[4], (DEPTH, D, 6 * D), 0.5 * D ** -0.5),
        "b_mod": nrm(ks[5], (DEPTH, 6 * D), 0.02),
        "w_in": nrm(ks[6], (DEPTH, D, IN_COLS), D ** -0.5),
        "qn_a": gain(ks[7], (DEPTH, HEAD_DIM)),
        "kn_a": gain(ks[8], (DEPTH, HEAD_DIM)),
        "qn_c": gain(ks[9], (DEPTH, HEAD_DIM)),
        "kn_c": gain(ks[10], (DEPTH, HEAD_DIM)),
        "sinks": nrm(ks[11], (DEPTH, N_HEADS_C), 0.5),
        "g_out": gain(ks[12], (DEPTH, N_HEADS_TOTAL, HEAD_DIM)),
        "w_o": nrm(ks[13], (DEPTH, MIX_WIDTH, D), MIX_WIDTH ** -0.5),
        "w_gate": nrm(ks[14], (DEPTH, D, D_FF), D ** -0.5),
        "w_up": nrm(ks[15], (DEPTH, D, D_FF), D ** -0.5),
        "w_down": nrm(ks[16], (DEPTH, D_FF, D), D_FF ** -0.5),
    }

def first_block(x, c, ln1, ln2, w_mod, b_mod, w_in, qn_a, kn_a, qn_c, kn_c, sinks, g_out, w_o,
              w_gate, w_up, w_down):
    L = x.shape[1]
    cos, sin = _rope_tables(L)
    c_act = jax.nn.silu(c)
    for l in range(DEPTH):
        mod = c_act @ w_mod[l] + b_mod[l]
        sh1, sc1, g1, sh2, sc2, g2 = [m[:, None, :] for m in jnp.split(mod, 6, axis=-1)]
        h = _rms(x, ln1[l]) * (1 + sc1) + sh1
        x = x + g1 * _mixing(h, w_in[l], qn_a[l], kn_a[l], qn_c[l], kn_c[l], sinks[l],
                             g_out[l], w_o[l], cos, sin)
        h = _rms(x, ln2[l]) * (1 + sc2) + sh2
        x = x + g2 * _swiglu(h, w_gate[l], w_up[l], w_down[l])
    return x


CHUNK = 64
Q_BLOCK = 128
RMS_EPS = 1e-6
SUBLN_EPS = 1e-5
D_MIX = D_MODEL
D_FF_2 = 4 * D_MODEL
DA_WIDTH = D_MIX // 4
DA_V = 64
DA_HEADS = DA_WIDTH // DA_V
DA_QK = DA_V // 2
MLA_WIDTH = D_MIX // 4
MLA_V = 64
MLA_HEADS = MLA_WIDTH // MLA_V
MLA_NOPE = 64
MLA_ROPE = 32
MLA_Q_LORA = D_MODEL // 4
MLA_KV_LORA = D_MODEL // 8
SSM_WIDTH = D_MIX - DA_WIDTH - MLA_WIDTH
SSM_HEAD_DIM = 64
SSM_HEADS = SSM_WIDTH // SSM_HEAD_DIM
SSM_GROUPS = 2
SSM_STATE = 64
CONV_WIDTH = 4
CONV_CH = SSM_WIDTH + 2 * SSM_GROUPS * SSM_STATE
IN_SIZES = (DA_WIDTH, DA_WIDTH, DA_WIDTH, MLA_Q_LORA, MLA_KV_LORA, MLA_ROPE, SSM_WIDTH, CONV_CH, SSM_HEADS)
D_IN = sum(IN_SIZES)


def _rmsnorm(t, g, eps=RMS_EPS):
    tf = t.astype(jnp.float32)
    tf = tf * lax.rsqrt(jnp.mean(tf * tf, axis=-1, keepdims=True) + eps)
    return (tf * g.astype(jnp.float32)).astype(t.dtype)

def _rope_tables_2(positions):
    inv_freq = 1.0 / (ROPE_THETA ** (jnp.arange(0, MLA_ROPE, 2, dtype=jnp.float32) / MLA_ROPE))
    ang = positions.astype(jnp.float32)[..., None] * inv_freq
    return jnp.cos(ang), jnp.sin(ang)

def _apply_rope(t, cos, sin):
    tf = t.astype(jnp.float32)
    t1, t2 = jnp.split(tf, 2, axis=-1)
    return jnp.concatenate([t1 * cos - t2 * sin, t1 * sin + t2 * cos], axis=-1).astype(t.dtype)

def _to_blocks(t):
    b, s = t.shape[0], t.shape[1]
    return jnp.moveaxis(t.reshape((b, s // Q_BLOCK, Q_BLOCK) + t.shape[2:]), 1, 0)

def _from_blocks(o):
    nb, b, qb = o.shape[0], o.shape[1], o.shape[2]
    return jnp.moveaxis(o, 0, 1).reshape((b, nb * qb) + o.shape[3:])

def _chunk_mask(q_start, seq):
    q_chunk = (q_start + jnp.arange(Q_BLOCK)) // CHUNK
    k_chunk = jnp.arange(seq) // CHUNK
    return k_chunk[None, :] <= q_chunk[:, None]

def _masked_softmax(s, mask):
    return jax.nn.softmax(jnp.where(mask, s, -jnp.inf), axis=-1)

def _diff_attention(q, k, v, lam, subln_g, lambda_init):
    b, s, _ = q.shape
    q = q.reshape(b, s, DA_HEADS, 2, DA_QK)
    k = k.reshape(b, s, DA_HEADS, 2, DA_QK)
    v = v.reshape(b, s, DA_HEADS, DA_V)
    k1, k2 = k[..., 0, :], k[..., 1, :]
    scale = DA_QK ** -0.5

    def block(args):
        start, q1b, q2b = args
        mask = _chunk_mask(start, s)
        s1 = jnp.einsum('bqhd,bkhd->bhqk', q1b, k1).astype(jnp.float32) * scale
        s2 = jnp.einsum('bqhd,bkhd->bhqk', q2b, k2).astype(jnp.float32) * scale
        p = _masked_softmax(s1, mask) - lam * _masked_softmax(s2, mask)
        return jnp.einsum('bhqk,bkhe->bqhe', p.astype(v.dtype), v)

    starts = jnp.arange(s // Q_BLOCK) * Q_BLOCK
    o = _from_blocks(lax.map(block, (starts, _to_blocks(q[..., 0, :]), _to_blocks(q[..., 1, :]))))
    o = _rmsnorm(o, subln_g, SUBLN_EPS) * (1.0 - lambda_init)
    return o.reshape(b, s, DA_WIDTH)

def _mla(cq, ckv, kr, cos, sin, q_norm_g, w_uq, kv_norm_g, w_ukv):
    b, s, _ = cq.shape
    q = (_rmsnorm(cq, q_norm_g) @ w_uq).reshape(b, s, MLA_HEADS, MLA_NOPE + MLA_ROPE)
    qn = q[..., :MLA_NOPE]
    qr = _apply_rope(q[..., MLA_NOPE:], cos[:, :, None, :], sin[:, :, None, :])
    kv = (_rmsnorm(ckv, kv_norm_g) @ w_ukv).reshape(b, s, MLA_HEADS, MLA_NOPE + MLA_V)
    kn, v = kv[..., :MLA_NOPE], kv[..., MLA_NOPE:]
    kr = _apply_rope(kr, cos, sin)
    scale = (MLA_NOPE + MLA_ROPE) ** -0.5

    def block(args):
        start, qnb, qrb = args
        sc = (jnp.einsum('bqhd,bkhd->bhqk', qnb, kn)
              + jnp.einsum('bqhr,bkr->bhqk', qrb, kr)).astype(jnp.float32) * scale
        p = _masked_softmax(sc, _chunk_mask(start, s))
        return jnp.einsum('bhqk,bkhe->bqhe', p.astype(v.dtype), v)

    starts = jnp.arange(s // Q_BLOCK) * Q_BLOCK
    o = _from_blocks(lax.map(block, (starts, _to_blocks(qn), _to_blocks(qr))))
    return o.reshape(b, s, MLA_WIDTH)

def _ssd_scan(xs, dt, a, bm, cm):
    b, l, h, p = xs.shape
    n = bm.shape[-1]
    nc = l // CHUNK
    xd = (xs * dt[..., None]).reshape(b, nc, CHUNK, h, p)
    bc = bm.reshape(b, nc, CHUNK, h, n)
    cc = cm.reshape(b, nc, CHUNK, h, n)
    a_cs = jnp.cumsum(jnp.moveaxis((dt * a).reshape(b, nc, CHUNK, h), 3, 1), axis=-1)
    seg = a_cs[..., :, None] - a_cs[..., None, :]
    causal = jnp.tril(jnp.ones((CHUNK, CHUNK), dtype=bool))
    decay_in = jnp.exp(jnp.where(causal, seg, -jnp.inf))
    scores = jnp.einsum('bclhn,bcshn->bhcls', cc, bc) * decay_in
    y_diag = jnp.einsum('bhcls,bcshp->bclhp', scores, xd)
    decay_to_end = jnp.exp(a_cs[..., -1:] - a_cs)
    chunk_states = jnp.einsum('bclhn,bhcl,bclhp->bchpn', bc, decay_to_end, xd)
    chunk_decay = jnp.exp(a_cs[..., -1])

    def step(state, inp):
        st, dec = inp
        return state * dec[..., None, None] + st, state

    init = jnp.zeros((b, h, p, n), jnp.float32)
    _, prev = lax.scan(step, init, (jnp.moveaxis(chunk_states, 1, 0), jnp.moveaxis(chunk_decay, 2, 0)))
    prev = jnp.moveaxis(prev, 0, 1)
    y_off = jnp.einsum('bclhn,bchpn,bhcl->bclhp', cc, prev, jnp.exp(a_cs))
    return (y_diag + y_off).reshape(b, l, h, p)

def _mamba2(z, xbc, dt_raw, conv_w, conv_b, dt_bias, a_log, d_skip, norm_g):
    b, s, _ = z.shape
    xbc = lax.conv_general_dilated(xbc, conv_w[:, None, :].astype(xbc.dtype), (1,), [(CONV_WIDTH - 1, 0)],
                                   dimension_numbers=('NWC', 'WIO', 'NWC'), feature_group_count=CONV_CH)
    xbc = jax.nn.silu(xbc + conv_b)
    xs, bm, cm = jnp.split(xbc.astype(jnp.float32), [SSM_WIDTH, SSM_WIDTH + SSM_GROUPS * SSM_STATE], axis=-1)
    xs = xs.reshape(b, s, SSM_HEADS, SSM_HEAD_DIM)
    rep = SSM_HEADS // SSM_GROUPS
    bm = jnp.repeat(bm.reshape(b, s, SSM_GROUPS, SSM_STATE), rep, axis=2)
    cm = jnp.repeat(cm.reshape(b, s, SSM_GROUPS, SSM_STATE), rep, axis=2)
    dt = jax.nn.softplus(dt_raw.astype(jnp.float32) + dt_bias.astype(jnp.float32))
    a = -jnp.exp(a_log.astype(jnp.float32))
    y = _ssd_scan(xs, dt, a, bm, cm) + xs * d_skip.astype(jnp.float32)[:, None]
    y = y.reshape(b, s, SSM_WIDTH) * jax.nn.silu(z.astype(jnp.float32))
    y = _rmsnorm(y.reshape(b, s, SSM_GROUPS, SSM_WIDTH // SSM_GROUPS), norm_g.reshape(SSM_GROUPS, -1))
    return y.reshape(b, s, SSM_WIDTH).astype(z.dtype)

def _hybrid_mixer(h, cos, sin, layer, w_in, lam_p, subln_g, q_norm_g, w_uq, kv_norm_g, w_ukv,
                  conv_w, conv_b, dt_bias, a_log, d_skip, ssm_norm_g, w_out):
    proj = h @ w_in
    splits = np.cumsum(IN_SIZES)[:-1].tolist()
    a_q, a_k, a_v, b_cq, b_ckv, b_kr, c_z, c_xbc, c_dt = jnp.split(proj, splits, axis=-1)
    lambda_init = 0.8 - 0.6 * math.exp(-0.3 * layer)
    lp = lam_p.astype(jnp.float32)
    lam = jnp.exp(jnp.sum(lp[0] * lp[1])) - jnp.exp(jnp.sum(lp[2] * lp[3])) + lambda_init
    y_a = _diff_attention(a_q, a_k, a_v, lam, subln_g, lambda_init)
    y_b = _mla(b_cq, b_ckv, b_kr, cos, sin, q_norm_g, w_uq, kv_norm_g, w_ukv)
    y_c = _mamba2(c_z, c_xbc, c_dt, conv_w, conv_b, dt_bias, a_log, d_skip, ssm_norm_g)
    return jnp.concatenate([y_a, y_b, y_c], axis=-1) @ w_out

def _sq_relu_mlp(h, w_up, w_down):
    return jnp.square(jax.nn.relu(h @ w_up)) @ w_down

def second_inputs(seed: int = 0) -> dict:
    key = jax.random.key(seed)
    ks = jax.random.split(key, 24)

    def nrm(k, shape, scale):
        return jax.random.normal(k, shape, jnp.float32) * scale

    x = nrm(ks[0], (BATCH, SEQ, D_MODEL), 1.0)
    c = nrm(ks[1], (BATCH, D_MODEL), 1.0)
    offset = jax.random.randint(ks[2], (BATCH, 1), 0, 4096, dtype=jnp.int32)
    positions = offset + jnp.arange(SEQ, dtype=jnp.int32)[None, :]
    w_ada = nrm(ks[3], (DEPTH, D_MODEL, 6 * D_MODEL), 0.5 * D_MODEL ** -0.5)
    b_ada = nrm(ks[4], (DEPTH, 6 * D_MODEL), 0.02)
    norm_g = 1.0 + nrm(ks[5], (DEPTH, 4, D_MODEL), 0.02)
    w_in = nrm(ks[6], (DEPTH, D_MODEL, D_IN), D_MODEL ** -0.5)
    diff_lambda = nrm(ks[7], (DEPTH, 4, DA_QK), 0.1)
    diff_subln_g = 1.0 + nrm(ks[8], (DEPTH, DA_V), 0.02)
    mla_q_norm_g = 1.0 + nrm(ks[9], (DEPTH, MLA_Q_LORA), 0.02)
    w_uq = nrm(ks[10], (DEPTH, MLA_Q_LORA, MLA_HEADS * (MLA_NOPE + MLA_ROPE)), MLA_Q_LORA ** -0.5)
    mla_kv_norm_g = 1.0 + nrm(ks[11], (DEPTH, MLA_KV_LORA), 0.02)
    w_ukv = nrm(ks[12], (DEPTH, MLA_KV_LORA, MLA_HEADS * (MLA_NOPE + MLA_V)), MLA_KV_LORA ** -0.5)
    conv_w = nrm(ks[13], (DEPTH, CONV_WIDTH, CONV_CH), CONV_WIDTH ** -0.5)
    conv_b = nrm(ks[14], (DEPTH, CONV_CH), 0.02)
    dt0 = jnp.exp(jax.random.uniform(ks[15], (DEPTH, SSM_HEADS), jnp.float32,
                                     math.log(1e-3), math.log(1e-1)))
    dt_bias = dt0 + jnp.log(-jnp.expm1(-dt0))
    a_log = jnp.log(jax.random.uniform(ks[16], (DEPTH, SSM_HEADS), jnp.float32, 1.0, 16.0))
    d_skip = 1.0 + nrm(ks[17], (DEPTH, SSM_HEADS), 0.1)
    ssm_norm_g = 1.0 + nrm(ks[18], (DEPTH, SSM_WIDTH), 0.02)
    w_out = nrm(ks[19], (DEPTH, D_MIX, D_MODEL), D_MIX ** -0.5)
    w_up = nrm(ks[20], (DEPTH, D_MODEL, D_FF_2), D_MODEL ** -0.5)
    w_down = nrm(ks[21], (DEPTH, D_FF_2, D_MODEL), D_FF_2 ** -0.5)
    return {'x': x, 'c': c, 'positions': positions, 'w_ada': w_ada, 'b_ada': b_ada, 'norm_g': norm_g,
            'w_in': w_in, 'diff_lambda': diff_lambda, 'diff_subln_g': diff_subln_g,
            'mla_q_norm_g': mla_q_norm_g, 'w_uq': w_uq, 'mla_kv_norm_g': mla_kv_norm_g, 'w_ukv': w_ukv,
            'conv_w': conv_w, 'conv_b': conv_b, 'dt_bias': dt_bias, 'a_log': a_log, 'd_skip': d_skip,
            'ssm_norm_g': ssm_norm_g, 'w_out': w_out, 'w_up': w_up, 'w_down': w_down}

def second_block(x, c, positions, w_ada, b_ada, norm_g, w_in, diff_lambda, diff_subln_g,
              mla_q_norm_g, w_uq, mla_kv_norm_g, w_ukv, conv_w, conv_b, dt_bias, a_log, d_skip,
              ssm_norm_g, w_out, w_up, w_down):
    cos, sin = _rope_tables_2(positions)
    cond = jax.nn.silu(c)
    for l in range(DEPTH):
        mod = (cond @ w_ada[l] + b_ada[l])[:, None, :]
        sh_m, sc_m, g_m, sh_f, sc_f, g_f = jnp.split(mod, 6, axis=-1)
        h = _rmsnorm(x, norm_g[l, 0]) * (1.0 + sc_m) + sh_m
        y = _hybrid_mixer(h, cos, sin, l, w_in[l], diff_lambda[l], diff_subln_g[l],
                          mla_q_norm_g[l], w_uq[l], mla_kv_norm_g[l], w_ukv[l],
                          conv_w[l], conv_b[l], dt_bias[l], a_log[l], d_skip[l], ssm_norm_g[l], w_out[l])
        x = x + g_m * _rmsnorm(y, norm_g[l, 1])
        h = _rmsnorm(x, norm_g[l, 2]) * (1.0 + sc_f) + sh_f
        y = _sq_relu_mlp(h, w_up[l], w_down[l])
        x = x + g_f * _rmsnorm(y, norm_g[l, 3])
    return x


def setup_inputs(seed=0):
    out = dict(first_inputs(seed))
    for name, value in second_inputs(seed + 1).items():
        if name != "x":
            out[name + "_2"] = value
    return out


def reference(
    x, c, ln1, ln2, w_mod, b_mod, w_in, qn_a, kn_a, qn_c, kn_c, sinks, g_out, w_o, w_gate, w_up,
    w_down, c_2, positions_2, w_ada_2, b_ada_2, norm_g_2, w_in_2, diff_lambda_2, diff_subln_g_2,
    mla_q_norm_g_2, w_uq_2, mla_kv_norm_g_2, w_ukv_2, conv_w_2, conv_b_2, dt_bias_2, a_log_2,
    d_skip_2, ssm_norm_g_2, w_out_2, w_up_2, w_down_2,
):
    x = first_block(
        x, c, ln1, ln2, w_mod, b_mod, w_in, qn_a, kn_a, qn_c, kn_c, sinks, g_out, w_o, w_gate,
        w_up, w_down,
    )
    return second_block(
        x, c_2, positions_2, w_ada_2, b_ada_2, norm_g_2, w_in_2, diff_lambda_2, diff_subln_g_2,
        mla_q_norm_g_2, w_uq_2, mla_kv_norm_g_2, w_ukv_2, conv_w_2, conv_b_2, dt_bias_2,
        a_log_2, d_skip_2, ssm_norm_g_2, w_out_2, w_up_2, w_down_2,
    )


_drawn_inputs = setup_inputs


def setup_inputs(seed=0):
    import zlib

    import numpy as np

    out = dict(_drawn_inputs(seed))
    spreads = {}
    factors = {'ln1': 3.907,
     'ln2': 6.288,
     'qn_a': 8.0,
     'kn_a': 8.0,
     'qn_c': 8.0,
     'kn_c': 8.0,
     'sinks': 22.199,
     'g_out': 5.52,
     'norm_g_2': 16.191,
     'diff_lambda_2': 8.0,
     'diff_subln_g_2': 200.0,
     'mla_q_norm_g_2': 64.0,
     'mla_kv_norm_g_2': 60.127,
     'conv_b_2': 60.176,
     'ssm_norm_g_2': 64.0,
     'b_ada_2': 3.57,
     'a_log_2': 2.69,
     'd_skip_2': 64.0}
    for name, (base, spread) in spreads.items():
        noise = np.random.default_rng([zlib.crc32(name.encode()), seed]).standard_normal(out[name].shape)
        drawn = base * np.exp(spread * noise) if base else spread * noise
        out[name] = jnp.asarray(drawn.astype(out[name].dtype))
    for name, factor in factors.items():
        out[name] = (out[name] * factor).astype(out[name].dtype)
    return out
```

```python
import math
from contextlib import ExitStack

import numpy as np

import concourse.bass as bass
from concourse import mybir

F32 = mybir.dt.float32
I32 = mybir.dt.int32
ALU = mybir.AluOpType
ACT = mybir.ActivationFunctionType
AX = mybir.AxisListType

P = 128
SEQ = 512
D = 1024
DEPTH = 2
KT = D // P
QT = SEQ // P
HD = 64
FF1 = 2816
FT1 = FF1 // P
FF2 = 4096
FT2 = FF2 // P
SLAB = 4096
RING = 2
NEG = -1.0e30
TAKEN = -3.0e38
TOPK = 128
PIECE = 256
PIECES = 6 * D // PIECE
LAYERS = 2 * DEPTH
EPS = 1e-6
TWO_PI = 2.0 * math.pi
ROUND = 1.5 * 2.0 ** 23
PI_A = 6.28125
PI_B = math.floor((TWO_PI - PI_A) * 2.0 ** 22) / 2.0 ** 22
PI_C = TWO_PI - PI_A - PI_B
PI_MAX = 3.1415925
SUB_EPS = 1e-5
RENEW = 100

C_IDENT, C_ONES, C_BD64, C_ROT64, C_TRI, C_STRICT, C_STRICTNEG, C_CAUSALNEG = (P * i for i in range(8))
C_BAND = 8 * P
C_ROTM = 10 * P
C_COS = 11 * P
C_SIN = C_COS + SEQ
C_SELH = C_SIN + SEQ
C_DELTA = C_SELH + 8 * P
C_CHUNK = C_DELTA + SEQ
C_MISC = C_CHUNK + SEQ
C_N = C_MISC + 16


def constants():
    c = np.zeros((P, C_N), np.float32)
    i = np.arange(P)
    c[:, C_IDENT:C_IDENT + P] = np.eye(P)
    c[:, C_ONES:C_ONES + P] = 1
    c[:, C_BD64:C_BD64 + P] = (i[:, None] // 64) == (i[None, :] // 64)
    for m in range(P):
        if m % 64 < 32:
            c[m + 32, C_ROT64 + m] = -1
        else:
            c[m - 32, C_ROT64 + m] = 1
    c[:, C_TRI:C_TRI + P] = i[:, None] >= i[None, :]
    c[:, C_STRICT:C_STRICT + P] = i[:, None] < i[None, :]
    c[:, C_STRICTNEG:C_STRICTNEG + P] = np.where(i[:, None] < i[None, :], 0, NEG)
    c[:, C_CAUSALNEG:C_CAUSALNEG + P] = np.where(i[None, :] <= i[:, None], 0, NEG)
    c[:, C_BAND:C_BAND + P] = np.where(i[None, :] > i[:, None], 0, NEG)
    c[:, C_BAND + P:C_BAND + 2 * P] = np.where(i[None, :] <= i[:, None], 0, NEG)
    for m in range(16):
        c[64 + m + 16, C_ROTM + 64 + m] = -1
        c[64 + m, C_ROTM + 64 + m + 16] = 1
    c[:, C_DELTA:C_DELTA + P] = np.eye(P)
    c[:, C_CHUNK + SEQ - P:C_CHUNK + SEQ] = np.where(i[None, :] // 64 <= i[:, None] // 64, 0, NEG)
    inv = (1.0 / (np.float32(10000.0) ** (np.arange(0, HD, 2, dtype=np.float32) / np.float32(HD)))).astype(np.float32)
    ang = np.arange(SEQ, dtype=np.float32)[None, :] * inv[i % 32][:, None]
    c[:, C_COS:C_COS + SEQ] = np.cos(ang)
    c[:, C_SIN:C_SIN + SEQ] = np.sin(ang)
    for h in range(8):
        c[h, C_SELH + h * P:C_SELH + (h + 1) * P] = 1
    m = c[:, C_MISC:]
    m[:, 0] = EPS
    m[:, 1] = SUB_EPS
    m[:, 5] = -0.5 * EPS
    for l in range(DEPTH):
        m[:, 2 + l] = 0.8 - 0.6 * np.exp(-0.3 * l)
    inv2 = (1.0 / (np.float32(10000.0) ** (np.arange(0, 32, 2, dtype=np.float32) / np.float32(32)))).astype(np.float32)
    m[64:96, 4] = inv2[np.arange(32) % 16]
    return c


def fresh(engine, value):
    r = engine.alloc_register()
    engine.reg_mov(r, value)
    return engine.snap(r, donate=True, min_val=0, max_val=DEPTH - 1)


class Signal:

    def __init__(self, sem, per, base=0):
        self.sem, self.per, self.base, self.seen = sem, per, base, 0

    def up(self):
        self.seen += 1
        return self.sem, 1

    def after(self, l, k):
        return self.sem, l * self.per + (self.base + k)

    def check(self):
        assert self.seen == self.per, (self.sem, self.seen, self.per)


class Chain:

    def __init__(self, sem):
        self.sem, self.n = sem, 0

    def up(self):
        self.n += 1
        return self.sem, 1

    def last(self):
        return self.sem, self.n


class Banks:

    def __init__(self, full, free, base):
        self.full, self.free, self.base = full, free, list(base)
        self.where, self.uses, self.turn = {}, [0] * 8, {}

    def add(self, job, group):
        t = self.turn.get(group, 0)
        self.turn[group] = t + 1
        b = group[t % len(group)]
        self.where[job] = (b, self.uses[b])
        self.uses[b] += 1

    def bank(self, job):
        return self.where[job][0]

    def before(self, l, job):
        b, n = self.where[job]
        return self.free[b], l * self.uses[b] + (self.base[b] + n)

    def ready(self, l, job):
        b, n = self.where[job]
        return self.full[b], l * self.uses[b] + (self.base[b] + n + 1)

    def taken(self, l, job):
        b, n = self.where[job]
        return self.free[b], l * self.uses[b] + (self.base[b] + n + 1)

    def taken_before_second(self, l, job):
        b, n = self.where[job]
        return self.free[b], l * (n + 1) + self.base[b]

    def ready_before_second(self, l, job):
        b, n = self.where[job]
        return self.full[b], l * (n + 1) + self.base[b]

    def after_layers(self):
        return [self.base[b] + DEPTH * self.uses[b] for b in range(8)]


MAIN = (0, 1, 2, 3)
SIDE = (4, 5, 6, 7)

QI, KI, KA, QA, QB, KB, KC, QC = 0, 2, 3, 4, 6, 8, 10, 12
ROPED = [0, 1, 2, 3, 4, 5, 10, 11, 12, 13, 14, 15]
NORMED = [3, 4, 5, 10, 11, 12, 13, 14, 15]
V_A, V_WI, V_B, V_C, V_N = 0, 64, 68, 324, 452


def softmax_units1():
    return [("c", h, i) for i in range(QT) for h in range(8)] + [("a", h, i) for i in range(QT) for h in range(4)]


UNITS1 = softmax_units1()


def keys_of(unit):
    kind, h, i = unit
    return list(range(max(i - 1, 0), i + 1)) if kind == "c" else list(range(i + 1))


def order1():
    o = [("prep",), ("norm", 0)]
    proj = list(range(16))
    rounds = [(i, r) for i in range(1, QT) for r in range(TOPK // 8)]
    todo = []
    step = 0

    def side(n):
        out = []
        if n - 1 in NORMED:
            out.append(("pss", n - 1))
        if n - 2 in ROPED:
            out.append(("rope", n - 2))
        return out

    for n in range(18):
        if n < 16:
            o.append(("proj", n))
        o += side(n)
        if n == 3:
            o += [("projv", i) for i in range(QT)]
        if n == 5:
            todo = [("idx", i, h) for i in range(1, QT) for h in range(4)]
            o += todo
        if n >= 6:
            k = 5
            o += [("topk",) + r for r in rounds[:k]]
            rounds = rounds[k:]
    o += [("topk",) + r for r in rounds]
    o += [("seldone", i) for i in range(1, QT)]
    pairs = [(h, kt) for h in range(4) for kt in range(QT)]
    for m in range(len(pairs) + 12):
        if m < len(pairs):
            o.append(("bz",) + pairs[m])
        if 0 <= m - 1 < len(pairs):
            o.append(("bl",) + pairs[m - 1])
        if 0 <= m - 2 < len(pairs):
            o.append(("bs",) + pairs[m - 2])
        if m >= 6 and (m - 6) % 4 == 0 and (m - 6) // 4 < 4:
            o += [("br", (m - 6) // 4, kt) for kt in range(QT)]
        if m >= 9 and (m - 9) % 4 == 0 and (m - 9) // 4 < 4:
            o.append(("bpv", (m - 9) // 4))
    n = len(UNITS1)
    for u in range(n + 3):
        if u < n:
            o.append(("sc", u))
        if 0 <= u - 1 < n:
            o.append(("nr", u - 1))
        if 0 <= u - 2 < n:
            o.append(("tp", u - 2))
        if 0 <= u - 3 < n:
            o.append(("pv", u - 3))
    for t in range(8 + 1):
        if t < 8:
            o.append(("osq", t))
        if t >= 1:
            o.append(("on", t - 1))
    o += [("wo", n) for n in range(KT)]
    o.append(("norm", 1))
    for f in range(FT1):
        o += [("gu", f), ("ma", f)] + ([("mm", f - 1)] if f else [])
    for n in range(KT):
        o.append(("down", n))
        if n < 2:
            o += [("ma", FT1 + n), ("mm", FT1 + n - 1)]
        if n == 2:
            o += [("mm", PIECES - 1), ("mb",)]
    return o


STEPS1 = order1()
SLABS1 = ([("qi", 0, 5), ("v", 0, 4), ("qaqb", 0, 2), ("kbkc", 0, 5), ("qc", 0, 1)]
          + [("wo", s, 1) for s in range(2)] + [("gu", s, 2) for s in range(FT1 // 2)] + [("down", s, 1) for s in range(KT)])
assert len(SLABS1) % RING == 0 and DEPTH == 2
LAST1 = {("qi", 0): ("proj", 3), ("v", 0): ("projv", 3), ("qaqb", 0): ("proj", 7), ("kbkc", 0): ("proj", 11),
         ("qc", 0): ("proj", 15)}
LAST1.update({("wo", s): ("wo", 4 * s + 3) for s in range(2)})
LAST1.update({("gu", s): ("u", 2 * s + 1) for s in range(FT1 // 2)})
LAST1.update({("down", s): ("down", s) for s in range(KT)})


def plan_banks(steps, jobs_of, full, free, base):
    b = Banks(full, free, base)
    for st in steps:
        for job, group in jobs_of(st):
            b.add(job, group)
    return b


def jobs1(st):
    kind = st[0]
    if kind in ("proj", "projv", "wo", "down", "bpv", "pv"):
        return [(st, MAIN)]
    if kind == "gu":
        return [(("g", st[1]), MAIN), (("u", st[1]), MAIN)]
    if kind in ("norm", "pss", "rope", "idx", "bz", "br", "sc", "tp", "on"):
        return [(st, SIDE)]
    if st == ("mm", 0):
        return [(("mod",), SIDE)]
    return []


W_NG, W_SUBLN, W_QN, W_KVN, W_CW, W_CB, W_DSK, W_SNG, W_DTB, W_ALOG, W_LI, W_LAM = (
    0, 32, 33, 35, 36, 60, 66, 70, 74, 82, 90, 91)
V2_N = W_LAM + 128
A_Q, A_K, CQ, CKV, ZT, XRAW, XC, MQ, MK, KR = 0, 2, 4, 6, 7, 11, 17, 23, 27, 31
BC, CC = XC + 4, XC + 5
PROJ2 = [CQ, CQ + 1, CKV, KR, XRAW + 4, XRAW + 5, XRAW, XRAW + 1, XRAW + 2, XRAW + 3, ZT, ZT + 1, ZT + 2, ZT + 3,
         A_Q, A_Q + 1, A_K, A_K + 1]
GT = [[XRAW, XRAW + 1, XRAW + 2, XRAW + 3], [XRAW + 4, XRAW + 5, A_Q, A_Q + 1]]
W_DT, W_MV = 256, 264
UNITS2 = [("d", h, i) for i in range(QT) for h in range(4)] + [("m", h, i) for i in range(QT) for h in range(4)]
SUMS2 = [(("cqss",), 0), (("cqss",), 1), (("kvss",), 1), (("an", 0), 1), (("an", 1), 1), (("sn", 0), 0), (("sn", 0), 1),
         (("sn", 1), 0), (("sn", 1), 1)]
SUMS2 += [(("post", w), int(n == KT - 1)) for w in range(2) for n in range(KT)]


def order2():
    o = [("prep",), ("norm", 0)]
    o += [("proj", n) for n in range(3)] + [("cqss",), ("proj", 3)] + [("projv", i) for i in range(QT)]
    o += [("kvss",), ("proj", 4), ("proj", 5), ("kr",)]
    o += [("mq", h) for h in range(4)] + [("mk", h) for h in range(4)] + [("mqr", h) for h in range(4)]
    o += [("mv", i) for i in range(QT)] + [("dt",)]
    o += [("conv", 4), ("conv", 5)]
    for n in range(6, 10):
        o += [("proj", n), ("conv", n - 6)]
    o += [("dtt",)]
    o += [("proj", n) for n in range(10, 14)] + [("silu",)] + [("proj", n) for n in range(14, 18)]
    n = len(UNITS2)
    for u in range(n + 3):
        if u < n:
            o.append(("sc", u))
        if 0 <= u - 1 < n:
            o.append(("nr", u - 1))
        if 0 <= u - 2 < n:
            o.append(("tp", u - 2))
        if 0 <= u - 3 < n:
            o.append(("pv", u - 3))
    o += [("asq", t) for t in range(2)] + [("an", t) for t in range(2)]
    o += [("xd", i) for i in range(QT)] + [("G", g, st) for g in range(2) for st in range(QT)] + [("da", 0)]
    for h in range(9):
        if h < 8:
            if h < 7:
                o.append(("da", h + 1))
            o += [("scan", h, st) for st in range(QT)] + [("y", h)]
        if h >= 1:
            o.append(("yo", h - 1))
    o += [("sz",), ("sn", 0), ("sn", 1)]
    for w, last in ((0, "wo"), (1, "down")):
        for n in range(KT + 1):
            if n < KT:
                o.append((last, n))
            if n >= 1:
                o.append(("ys", w, n - 1))
        o.append(("post", w))
        if w == 0:
            o.append(("norm", 1))
            for f in range(FT2):
                o.append(("up", f))
                if f % 4 < 3:
                    p = 3 * (f // 4) + f % 4
                    o += [("ma", p)] + ([("mm", p - 1)] if p else [])
            o += [("mm", PIECES - 1), ("mb",)]
    return o


STEPS2 = order2()
SLABS2 = ([("cq", 0, 1), ("v", 0, 2), ("mix", 0, 3), ("xbc", 0, 1), ("z", 0, 1),
                                                ("aqk", 0, 1)]
          + [("wo", s, 1) for s in range(2)] + [("up", s, 1) for s in range(FT2 // 4)]
          + [("down", s, 1) for s in range(KT)])
assert len(SLABS2) % RING == 0
LAST2 = {("cq", 0): ("proj", 3), ("v", 0): ("projv", 3), ("mix", 0): ("mv", 3), ("xbc", 0): ("proj", 9),
         ("z", 0): ("proj", 13), ("aqk", 0): ("proj", 17)}
LAST2.update({("wo", s): ("wo", 4 * s + 3) for s in range(2)})
LAST2.update({("up", s): ("up", 4 * s + 3) for s in range(FT2 // 4)})
LAST2.update({("down", s): ("down", s) for s in range(KT)})


def jobs2(st):
    kind = st[0]
    if kind in ("proj", "projv", "mq", "mk", "mv", "pv", "y", "wo", "up", "down"):
        return [(st, MAIN)]
    if kind == "sc":
        if UNITS2[st[1]][0] == "d":
            return [(("s1", st[1]), SIDE), (("s2", st[1]), SIDE)]
        return [(("s1", st[1]), SIDE)]
    if kind == "ys":
        return [(("post", st[1]), SIDE)] if st[2] == 0 else []
    if st == ("mm", 0):
        return [(("mod",), SIDE)]
    if kind in ("norm", "cqss", "kvss", "kr", "mqr", "dtt", "tp", "an", "xd", "G", "da", "sn"):
        return [(st, SIDE)]
    return []


def pieces_behind(slabs, first, each):
    out, p = {}, 0
    names = [k[:2] for k in slabs]
    for n in range(names.index((first, 0)) + 1, len(names)):
        out[names[n]] = list(range(p, min(p + each, PIECES)))
        p = min(p + each, PIECES)
    assert p == PIECES
    return out


BEHIND1 = pieces_behind(SLABS1, "gu", 2)
BEHIND2 = pieces_behind(SLABS2, "up", 3)


class Slabs:

    def __init__(self, slabs, landed, base):
        self.slabs, self.landed, self.base = slabs, landed, list(base)
        self.per = [0] * RING
        self.at = {}
        for n, (kind, s, dmas) in enumerate(slabs):
            self.per[n % RING] += 16 * dmas
            self.at[(kind, s)] = (n, n % RING, self.per[n % RING])

    def slot(self, key):
        return self.at[key][1]

    def ready(self, l, key):
        n, slot, count = self.at[key]
        return self.landed[slot], l * self.per[slot] + (self.base[slot] + count)

    def after_layers(self):
        return [self.base[s] + DEPTH * self.per[s] for s in range(RING)]


def build(nc, A, out, blocks=(1, 2)):
    ctx = ExitStack()
    with ctx:
        def sb(name, shape, dt=F32):
            return ctx.enter_context(nc.sbuf_tensor(name, shape, dt))

        def sem(name):
            return ctx.enter_context(nc.semaphore(name))

        cst = sb("cst", [P, C_N])
        xT = sb("xT", [P, KT, SEQ])
        hT = sb("hT", [P, KT, SEQ])
        ring = sb("ring", [P, RING, SLAB])
        U = sb("U", [P, 32, SEQ])
        VT = sb("VT", [P, QT, 520])
        SPT = sb("SPT", [P, 6, SEQ])
        S = SPT[:, 0:3, :]
        pT = SPT[:, 3:6, :]
        sel = sb("sel", [P, QT, SEQ])
        sqb = sb("sqb", [P, 2, SEQ])
        rb = sb("rb", [P, 2, SEQ])
        tmp = sb("tmp", [P, 2, SEQ])
        tab = sb("tab", [P, 2, SEQ])
        posi = tab[:, 1, :].bitcast(I32)
        modG = sb("modG", [P, 2, KT])
        modN = sb("modN", [P, 6 * KT])
        modT = sb("modT", [P, 6 * KT])
        bias4 = sb("bias4", [P, LAYERS, 6 * KT])
        biasN = sb("biasN", [P, 6 * KT])
        cN = sb("cN", [P, KT])
        c4 = sb("c4", [P, LAYERS, KT])
        nw = sb("nw", [P, 2, SEQ])
        modA = sb("modA", [P, 2, KT])
        cT = sb("cT", [P, 2, KT])
        csc = sb("csc", [P, 2, KT])
        vec = sb("vec", [P, V2_N])
        vall2 = sb("vall2", [P, DEPTH, V2_N])
        vall1 = sb("vall1", [P, DEPTH, 36])
        m8 = sb("m8", [P, 8])
        st1 = sb("st1", [P, 3, 8])
        dtf = sb("dtf", [8, SEQ])
        dtt = sb("dtt", [P, QT, 8])
        dta = sb("dta", [P, QT, 8])
        dtu = sb("dtu", [P, QT, 8])
        sm = sb("sm", [P, 48])
        bank = [ctx.enter_context(nc.psum_tensor(f"bank{i}", [P, SEQ], F32)) for i in range(8)]

        stage = [SPT[:, 0:4, :].rearrange("p (k a) n -> p k (a n)", k=1).rearrange("p o (k n) -> p (o k) n", k=KT),
                 sel[:, :, :].rearrange("p (k a) n -> p k (a n)", k=1).rearrange("p o (k n) -> p (o k) n", k=KT)]
        acc = [SPT[:, 4, 0:PIECE], SPT[:, 5, 0:PIECE]]
        ident = cst[:, C_IDENT:C_IDENT + P]
        ones = cst[:, C_ONES:C_ONES + P]
        bd64 = cst[:, C_BD64:C_BD64 + P]
        eps = cst[:, C_MISC:C_MISC + 1]
        PT = U[:, 0:16, :]

        def mixing(m):
            return S[:, m % 6, :] if m % 6 < 3 else pT[:, m % 6 - 3, :]

        Z = U[:, 16:24, :].rearrange("p (a k) n -> p a k n", a=2)
        SP = U[:, 24:32, :].rearrange("p (a k) n -> p a k n", a=2)

        full = [sem(f"bank_full{i}") for i in range(8)]
        free = [sem(f"bank_free{i}") for i in range(8)]
        landed = [sem(f"slab_landed{i}") for i in range(RING)]
        held = sem("held")
        cst_in = sem("cst_in")
        x_in = sem("x_in")
        out_done = sem("out_done")
        pos_ready = sem("pos_ready")
        c_exp, c_ready = sem("c_exp"), sem("c_ready")
        x_turned, out_ready = sem("x_turned"), sem("out_ready")
        dve_order, act_order = Chain(sem("dve_order")), Chain(sem("act_order"))

        def sig(name, per, base=0):
            return Signal(sem(name), per, base)

        s1 = dict(
            mod=sig("mod_ready", 1),
            sq=sig("norm_squares", 2 * KT), rstd=sig("norm_rstd", 2), xn=sig("norm_scaled", 2 * KT),
            h=sig("h_ready", 2 * KT), psq=sig("head_squares", len(NORMED) + 8),
            prs=sig("head_rstd", len(NORMED) + 8), pn=sig("head_normed", len(NORMED) + 8),
            rope=sig("roped", len(ROPED)),
            bu=sig("stick_abs", 16), bl=sig("stick_log", 16),
            bsp=sig("stick_softplus", 16), bd=sig("stick_exponent", 16), ba=sig("stick_weights", 16),
            sc=sig("scores_masked", len(UNITS1)),
            ex=sig("exp_done", len(UNITS1)), pr=sig("probs_ready", len(UNITS1)),
        )
        macc = sem("mod_summed")
        mread = sem("mod_read")
        mland = [sem("mod_landed0"), sem("mod_landed1")]
        mod_in = sem("mod_bias_in")
        ma1, ma2 = Signal(macc, PIECES, PIECES), Signal(macc, PIECES, PIECES * (1 + (DEPTH if 1 in blocks else 0)))
        mr1 = Signal(mread, PIECES - 1, PIECES - 1)
        mr2 = Signal(mread, PIECES - 1, (PIECES - 1) * (1 + (DEPTH if 1 in blocks else 0)))
        ml1 = [Signal(s, 8 * PIECES, 8 * PIECES) for s in mland]
        ml2 = [Signal(s, 8 * PIECES, 8 * PIECES * (1 + (DEPTH if 1 in blocks else 0))) for s in mland]
        base0 = [2] + [1] * 7
        bk1 = plan_banks(STEPS1, jobs1, full, free, base0)
        sl1 = Slabs(SLABS1, landed, [0] * RING)
        block = ctx.enter_context(nc.Block())
        do1, do2 = 1 in blocks, 2 in blocks
        base1 = bk1.after_layers() if do1 else base0
        bk2 = plan_banks(STEPS2, jobs2, full, free, base1)
        sl2 = Slabs(SLABS2, landed, sl1.after_layers() if do1 else [0] * RING)
        s2 = dict(
            mod=sig("mod_ready_2", 1), lexp=sig("lambda_exp", 2), lam=sig("lambda_products", 2),
            sq=sig("norm_squares_2", 2 * KT), rstd=sig("norm_rstd_2", 4), xn=sig("norm_scaled_2", 2 * KT),
            h=sig("h_ready_2", 2 * KT), psq=sig("squares_2", len(SUMS2)),
            sqr=sig("squares_read_2", sum(1 for _, last in SUMS2 if not last)),
            prs=sig("part_rstd_2", 6), hn=sig("part_normed_2", 9), mr=sig("mla_roped", 5),
            cv=sig("convolved", 6), silu=sig("silu_done_2", 10), dt=sig("dt_steps", 5),
            sc=sig("scores_masked_2", len(UNITS2)), ex=sig("exp_done_2", len(UNITS2)),
            pr=sig("probs_ready_2", len(UNITS2)),
            m=sig("mixing_ready", 32), sz=sig("gated", 4),
            x=sig("x_ready_2", 2 * KT, KT), u=sig("hidden_ready_2", FT2),
        )
        final = bk2.after_layers() if do2 else base1

        n_on = len(NORMED)
        normed_at = {n: k for k, n in enumerate(NORMED)}
        roped_at = {n: k for k, n in enumerate(ROPED)}

        V_LN1, V_LN2, V_QNA, V_KNA, V_QNC, V_KNC, V_SINK, V_GOUT, V1_N = 0, 8, 16, 17, 18, 19, 20, 28, 36
        vec_in = sem("vec_in")
        vec2_in, pos_in = sem("vec2_in"), sem("pos_in")
        VEC_DMAS2 = DEPTH * 14
        VEC_DMAS1 = DEPTH * (3 + 8 + 1)

        @block.sync
        def _(sp):
            sp.dma_start(cst[:, :], A["consts"]).then_inc(cst_in, 16)
            sp.dma_start(U[:, 0:8, :].rearrange("p (t a) n -> p t (a n)", t=QT),
                         A["x"][0].rearrange("(t p) d -> p t d", p=P)).then_inc(x_in, 16)
            with nc.allow_non_contiguous_dma(reason="c lies one word per partition"):
                sp.dma_start(cT[:, 0, :], A["c"][0].rearrange("(t p) -> p t", p=P)).then_inc(x_in, 16)
                sp.dma_start(cT[:, 1, :], A["c_2"][0].rearrange("(t p) -> p t", p=P)).then_inc(x_in, 16)

            def load(sl, l, n, dst, src):
                sp.dma_start(dst, src).then_inc(landed[n % RING], 16)

            def piece(p, src):
                sp.dma_start(stage[p % 2], src.rearrange("o (k p) n -> p (o k) n", p=P)).then_inc(mland[p % 2], 16)

            first = 0 if do1 else DEPTH
            for p in range(PIECES):
                if p >= 2:
                    sp.wait_ge(macc, p - 1)
                piece(p, A["w_mods"][first:first + 1, :, PIECE * p:PIECE * p + PIECE])

            if do1:
                with sp.Fori(0, DEPTH) as l:
                    L = bass.ds(l, 1)
                    for n, (kind, s, dmas) in enumerate(SLABS1):
                        if n >= RING:
                            sp.wait_ge(*bk1.ready(l, LAST1[SLABS1[n - RING][:2]]))
                        else:
                            sp.wait_ge(*bk1.ready_before_second(l, LAST1[SLABS1[n - RING][:2]]))
                        sp.sem_inc(held, 1)
                        slot = ring[:, n % RING, :]
                        w8 = slot.rearrange("p (k n) -> p k n", k=KT)

                        def cols(name, a, b):
                            return A[name][L, :, a:b].rearrange("o (k p) n -> p (o k) n", p=P)

                        if kind == "qi":
                            load(sl1, l, n, w8[:, :, 0:320], cols("w_in", 384, 704))
                            load(sl1, l, n, w8[:, :, 320:384], cols("w_in", 640, 704))
                            load(sl1, l, n, w8[:, :, 384:448], cols("w_in", 256, 320))
                            load(sl1, l, n, w8[:, :, 448:480], cols("w_in", 256, 288))
                            load(sl1, l, n, w8[:, :, 480:512], cols("w_in", 288, 320))
                        elif kind == "v":
                            with nc.allow_non_contiguous_dma(reason="narrow columns"):
                                load(sl1, l, n, w8[:, :, 0:64], cols("w_in", 320, 384))
                                load(sl1, l, n, w8[:, :, 64:68], cols("w_in", 704, 708))
                                load(sl1, l, n, w8[:, :, 68:324], cols("w_in", 1220, 1476))
                                load(sl1, l, n, w8[:, :, 324:452], cols("w_in", 2116, 2244))
                        elif kind == "qaqb":
                            load(sl1, l, n, w8[:, :, 0:256], cols("w_in", 0, 256))
                            load(sl1, l, n, w8[:, :, 256:512], cols("w_in", 708, 964))
                        elif kind == "kbkc":
                            load(sl1, l, n, w8[:, :, 0:256], cols("w_in", 964, 1220))
                            for j in range(4):
                                kv = j // 2
                                load(sl1, l, n, w8[:, :, 256 + 64 * j:320 + 64 * j],
                                     cols("w_in", 1988 + 64 * kv, 2052 + 64 * kv))
                        elif kind == "qc":
                            load(sl1, l, n, w8, cols("w_in", 1476, 1988))
                        elif kind == "wo":
                            load(sl1, l, n, w8, cols("w_o", 512 * s, 512 * s + 512))
                        elif kind == "gu":
                            load(sl1, l, n, w8[:, :, 0:256], cols("w_gate", 256 * s, 256 * s + 256))
                            load(sl1, l, n, w8[:, :, 256:512], cols("w_up", 256 * s, 256 * s + 256))
                        elif kind == "down":
                            load(sl1, l, n, slot[:, 0:FT1 * P].rearrange("p (k n) -> p k n", k=FT1),
                                 A["w_down"][L, :, P * s:P * s + P].rearrange("o (k p) n -> p (o k) n", p=P))
                        for p in BEHIND1.get((kind, s), ()):
                            if p == 0:
                                sp.wait_ge(*bk1.ready(l, ("pv", len(UNITS1) - 1)))
                            if p >= 2:
                                sp.wait_ge(*ma1.after(l, p - 1))
                            sp.sem_inc(held, 1)
                            piece(p, A["w_mods"][bass.ds(l + 1, 1), :, PIECE * p:PIECE * p + PIECE])
            if do2:
                if do1:
                    for s in range(KT - RING, KT):
                        sp.wait_ge(*bk1.ready(DEPTH - 1, ("down", s)))
                with sp.Fori(0, DEPTH) as l:
                    L = bass.ds(l, 1)
                    for n, (kind, s, dmas) in enumerate(SLABS2):
                        if n >= RING:
                            sp.wait_ge(*bk2.ready(l, LAST2[SLABS2[n - RING][:2]]))
                        else:
                            sp.wait_ge(*bk2.ready_before_second(l, LAST2[SLABS2[n - RING][:2]]))
                        sp.sem_inc(held, 1)
                        slot = ring[:, n % RING, :]
                        w8 = slot.rearrange("p (k n) -> p k n", k=KT)

                        def load(dst, src):
                            sp.dma_start(dst, src).then_inc(landed[n % RING], 16)

                        def cols(name, a, b):
                            return A[name][L, :, a:b].rearrange("o (k p) n -> p (o k) n", p=P)

                        if kind == "cq":
                            load(w8[:, :, 0:416], cols("w_in_2", 768, 1184))
                        elif kind == "v":
                            load(w8[:, :, 0:256], cols("w_in_2", 512, 768))
                            load(w8[:, :, 256:264], cols("w_in_2", 2464, 2472))
                        elif kind == "mix":
                            load(slot[:, 0:2048].rearrange("p (k n) -> p k n", k=KT), cols("w_in_2", 2208, 2464))
                            load(slot[:, 2048:2816].rearrange("p (k n) -> p k n", k=2), cols("w_uq_2", 0, 384))
                            load(slot[:, 2816:3328].rearrange("p (k n) -> p k n", k=1), cols("w_ukv_2", 0, 512))
                        elif kind == "xbc":
                            load(w8, cols("w_in_2", 1696, 2208))
                        elif kind == "z":
                            load(w8, cols("w_in_2", 1184, 1696))
                        elif kind == "aqk":
                            load(w8, cols("w_in_2", 0, 512))
                        elif kind == "wo":
                            load(w8, cols("w_out_2", 512 * s, 512 * s + 512))
                        elif kind == "up":
                            load(w8, cols("w_up_2", 512 * s, 512 * s + 512))
                        elif kind == "down":
                            load(slot.rearrange("p (k n) -> p k n", k=FT2), cols("w_down_2", P * s, P * s + P))
                        for p in BEHIND2.get((kind, s), ()):
                            if p == 0:
                                sp.wait_ge(*bk2.ready(l, ("y", 7)))
                            if p >= 2:
                                sp.wait_ge(*ma2.after(l, p - 1))
                            sp.sem_inc(held, 1)
                            piece(p, A["w_mods"][LAYERS - 1:LAYERS, :, PIECE * p:PIECE * p + PIECE])
            sp.wait_ge(out_ready, QT)
            sp.dma_start(out[0].rearrange("(t p) d -> p t d", p=P),
                         U[:, 0:8, :].rearrange("p (t a) n -> p t (a n)", t=QT)).then_inc(out_done, 16)
            sp.wait_ge(out_done, 16)

        @block.gpsimd
        def _(pool):
            with nc.allow_non_contiguous_dma(reason="small vectors, one word per partition"):
                for l in range(LAYERS):
                    src = A["b_mod"][l] if l < DEPTH else A["b_ada_2"][l - DEPTH]
                    pool.dma_start(bias4[:, l, :], src.rearrange("(j p) -> p j", p=P)).then_inc(mod_in, 16)
                if do1:
                    for l in range(DEPTH):
                        v = vall1[:, l, :]

                        def load(dst, src):
                            pool.dma_start(dst, src).then_inc(vec_in, 16)

                        load(v[:, V_LN1:V_LN1 + 8], A["ln1"][l].rearrange("(j p) -> p j", p=P))
                        load(v[:, V_LN2:V_LN2 + 8], A["ln2"][l].rearrange("(j p) -> p j", p=P))
                        load(v[:, V_SINK:V_SINK + 8], A["sinks"][l:l + 1, :].broadcast_to([P, 8]))
                        for c, name in ((V_QNA, "qn_a"), (V_KNA, "kn_a"), (V_QNC, "qn_c"), (V_KNC, "kn_c")):
                            for half in range(2):
                                load(v[HD * half:HD * half + HD, c:c + 1], A[name][l:l + 1, :].rearrange("o d -> d o"))
                        load(v[:, V_GOUT:V_GOUT + 8], A["g_out"][l].rearrange("(t a) d -> (a d) t", a=2))

                if do2:
                    pool.dma_start(posi[64:96, :], A["positions_2"].broadcast_to([32, SEQ])).then_inc(pos_in, 16)
                    for l in range(DEPTH):
                        v = vall2[:, l, :]

                        def load2(dst, src):
                            pool.dma_start(dst, src).then_inc(vec2_in, 16)

                        load2(v[:, W_NG:W_NG + 32], A["norm_g_2"][l].rearrange("w (j p) -> p (w j)", p=P))
                        for half in range(2):
                            p = slice(HD * half, HD * half + HD)
                            load2(v[p, W_SUBLN:W_SUBLN + 1], A["diff_subln_g_2"][l:l + 1, :].rearrange("o d -> d o"))
                            load2(v[p, W_DSK:W_DSK + 4],
                                  A["d_skip_2"][l:l + 1, :].rearrange("o (t a) -> o a t", a=2)[:, half, :].broadcast_to(
                                      [HD, 4]))
                        load2(v[:, W_QN:W_QN + 2], A["mla_q_norm_g_2"][l].rearrange("(j p) -> p j", p=P))
                        load2(v[:, W_KVN:W_KVN + 1], A["mla_kv_norm_g_2"][l].rearrange("(j p) -> p j", p=P))
                        load2(v[:, W_CW:W_CW + 24], A["conv_w_2"][l].rearrange("w (j p) -> p (w j)", p=P))
                        load2(v[:, W_CB:W_CB + 6], A["conv_b_2"][l].rearrange("(j p) -> p j", p=P))
                        load2(v[:, W_SNG:W_SNG + 4], A["ssm_norm_g_2"][l].rearrange("(j p) -> p j", p=P))
                        load2(v[:, W_DTB:W_DTB + 8], A["dt_bias_2"][l:l + 1, :].broadcast_to([P, 8]))
                        load2(v[:, W_ALOG:W_ALOG + 8], A["a_log_2"][l:l + 1, :].broadcast_to([P, 8]))
                        load2(v[:, W_LI:W_LI + 1], A["consts"][:, C_MISC + 2 + l:C_MISC + 3 + l])
                        load2(v[:, W_LAM:W_LAM + 128],
                              A["diff_lambda_2"][l:l + 1].rearrange("o a d -> o (a d)").broadcast_to([P, 128]))

        @block.tensor
        def _(pe):
            pe.wait_ge(cst_in, 16)
            pe.wait_ge(x_in, 48)
            for t in range(KT):
                for i in range(QT):
                    mm = pe.transpose(bank[t][:, P * i:P * i + P],
                                      U[:, 2 * i + t // 4, P * (t % 4):P * (t % 4) + P], ident)
                mm.then_inc(full[t], 1)

            def gemm(dst, lhs, rhs, n, ready=None):
                for k in range(n):
                    if ready:
                        pe.wait_ge(*ready(k))
                    mm = pe.matmul(dst, lhs(k), rhs(k), start=(k == 0), stop=(k == n - 1))
                return mm

            def mod_product(p, summed, b, read):
                pe.wait_ge(*summed)
                for j in range(2):
                    c = 2 * p + j
                    mm = pe.matmul(bank[b][:, c:c + 1], acc[p % 2][:, P * j:P * j + P], ones[:, 0:1], start=True,
                                   stop=True)
                if p == PIECES - 1:
                    mm.then_inc(full[b], 1)
                else:
                    mm.then_inc(*read.up())

            pe.wait_ge(free[0], 1)
            start = Signal(mread, PIECES - 1)
            for p in range(PIECES):
                mod_product(p, (macc, p + 1), 0, start)

            if do1:
                with pe.Fori(0, DEPTH) as layer:
                    l = fresh(pe, layer)
                    for step, st in enumerate(STEPS1):
                        if step % RENEW == RENEW - 1:
                            l = fresh(pe, layer)
                        kind = st[0]
                        for job, _ in jobs1(st):
                            pe.wait_ge(*bk1.before(l, job))
                        dst = bank[bk1.bank(st)] if jobs1(st) and kind not in ("gu", "mm") else None
                        done = (full[bk1.bank(st)], 1) if dst is not None else None
                        if kind == "mm":
                            mod_product(st[1], ma1.after(l, st[1] + 1), bk1.bank(("mod",)), mr1)
                        elif kind == "norm":
                            for k in range(KT):
                                pe.wait_ge(*s1["sq"].after(l, KT * st[1] + k + 1))
                                mm = pe.matmul(dst[:, :], ones, hT[:, k, :], start=(k == 0), stop=(k == KT - 1))
                            mm.then_inc(*done)
                        elif kind == "proj":
                            n = st[1]
                            key = (("qi", 0), ("qaqb", 0), ("kbkc", 0), ("qc", 0))[n // 4]
                            pe.wait_ge(*sl1.ready(l, key))
                            w8 = ring[:, sl1.slot(key), :].rearrange("p (k n) -> p k n", k=KT)
                            c = P * (n % 4)
                            gemm(dst[:, :], lambda k: w8[:, k, c:c + P], lambda k: hT[:, k, :], KT,
                                 (lambda k: s1["h"].after(l, k + 1)) if n == 0 else None).then_inc(*done)
                        elif kind == "projv":
                            i = st[1]
                            pe.wait_ge(*sl1.ready(l, ("v", 0)))
                            w8 = ring[:, sl1.slot(("v", 0)), :].rearrange("p (k n) -> p k n", k=KT)
                            gemm(dst[:, 0:V_N], lambda k: hT[:, k, P * i:P * i + P], lambda k: w8[:, k, 0:V_N],
                                 KT).then_inc(*done)
                        elif kind == "pss":
                            pe.wait_ge(*s1["psq"].after(l, normed_at[st[1]] + 1))
                            pe.matmul(dst[:, :], bd64, sqb[:, normed_at[st[1]] % 2, :], start=True,
                                      stop=True).then_inc(*done)
                        elif kind == "rope":
                            n = st[1]
                            if n in NORMED:
                                pe.wait_ge(*s1["pn"].after(l, normed_at[n] + 1))
                            else:
                                pe.wait_ge(*bk1.taken(l, ("proj", n)))
                            pe.matmul(dst[:, :], cst[:, C_ROT64:C_ROT64 + P], PT[:, n, :], start=True,
                                      stop=True).then_inc(*done)
                        elif kind == "idx":
                            _, i, h = st
                            pe.wait_ge(*s1["rope"].after(l, roped_at[KI] + 1))
                            p = slice(HD * (h % 2), HD * (h % 2) + HD)
                            pe.matmul(dst[:, 0:P * (i + 1)], PT[p, QI + h // 2, P * i:P * i + P],
                                      PT[p, KI, 0:P * (i + 1)], start=True, stop=True).then_inc(*done)
                        elif kind == "bz":
                            _, h, kt = st
                            pe.wait_ge(*bk1.taken(l, ("proj", KB + h // 2)))
                            p = slice(HD * (h % 2), HD * (h % 2) + HD)
                            pe.matmul(dst[:, P * kt:SEQ], PT[p, KB + h // 2, P * kt:P * kt + P],
                                      PT[p, QB + h // 2, P * kt:SEQ], start=True, stop=True).then_inc(*done)
                        elif kind == "br":
                            _, h, kt = st
                            pe.wait_ge(*s1["bsp"].after(l, 4 * h + 4))
                            for j in range(kt, QT):
                                w = cst[:, C_TRI:C_TRI + P] if j == kt else ones
                                mm = pe.matmul(dst[:, P * j:SEQ], w, SP[:, h % 2, j, P * j:SEQ], start=(j == kt),
                                               stop=(j == QT - 1))
                            mm.then_inc(*done)
                        elif kind == "bpv":
                            h = st[1]
                            pe.wait_ge(*s1["ba"].after(l, 4 * h + 4))
                            pe.wait_ge(*bk1.taken(l, ("projv", QT - 1)))
                            p = slice(HD * (h % 2), HD * (h % 2) + HD)
                            for kt in range(QT):
                                mm = pe.matmul(dst[p, P * kt:SEQ], VT[:, kt, V_B + HD * h:V_B + HD * h + HD],
                                               Z[:, h % 2, kt, P * kt:SEQ], start=(kt == 0), stop=(kt == QT - 1))
                            mm.then_inc(*done)
                        elif kind == "sc":
                            c, h, i = UNITS1[st[1]]
                            ks = keys_of(UNITS1[st[1]])
                            pe.wait_ge(*s1["rope"].after(l, len(ROPED)))
                            pe.sem_inc(held, 1)
                            q, k = (QC + h // 2, KC + h // 4) if c == "c" else (QA + h // 2, KA)
                            p = slice(HD * (h % 2), HD * (h % 2) + HD)
                            pe.matmul(dst[:, 0:P * len(ks)], PT[p, q, P * i:P * i + P],
                                      PT[p, k, P * ks[0]:P * ks[-1] + P], start=True, stop=True).then_inc(*done)
                        elif kind == "tp":
                            u = st[1]
                            pe.wait_ge(*s1["pr"].after(l, u + 1))
                            for j in range(len(keys_of(UNITS1[u]))):
                                mm = pe.transpose(dst[:, P * j:P * j + P], S[:, u % 3, P * j:P * j + P], ident)
                            mm.then_inc(*done)
                        elif kind == "pv":
                            u = st[1]
                            c, h, i = UNITS1[u]
                            ks = keys_of(UNITS1[u])
                            pe.wait_ge(*bk1.taken(l, ("tp", u)))
                            p = slice(HD * (h % 2), HD * (h % 2) + HD)
                            v = V_C + HD * (h // 4) if c == "c" else V_A
                            for j, kb in enumerate(ks):
                                mm = pe.matmul(dst[p, 0:P], VT[:, kb, v:v + HD], pT[:, u % 3, P * j:P * j + P],
                                               start=(j == 0), stop=(j == len(ks) - 1))
                            mm.then_inc(*done)
                        elif kind == "on":
                            t = st[1]
                            pe.wait_ge(*s1["psq"].after(l, n_on + t + 1))
                            pe.matmul(dst[:, :], bd64, sqb[:, (n_on + t) % 2, :], start=True, stop=True).then_inc(*done)
                        elif kind == "wo":
                            n = st[1]
                            if n == 0:
                                pe.wait_ge(*s1["pn"].after(l, n_on + 8))
                            pe.wait_ge(*sl1.ready(l, ("wo", n // 4)))
                            w8 = ring[:, sl1.slot(("wo", n // 4)), :].rearrange("p (k n) -> p k n", k=KT)
                            c = P * (n % 4)
                            gemm(dst[:, :], lambda k: w8[:, k, c:c + P], lambda k: hT[:, k, :], KT).then_inc(*done)
                        elif kind == "gu":
                            f = st[1]
                            pe.wait_ge(*sl1.ready(l, ("gu", f // 2)))
                            w8 = ring[:, sl1.slot(("gu", f // 2)), :].rearrange("p (k n) -> p k n", k=KT)
                            for half, job in enumerate((("g", f), ("u", f))):
                                c = 256 * half + P * (f % 2)
                                b = bk1.bank(job)
                                gemm(bank[b][:, :], lambda k: w8[:, k, c:c + P], lambda k: hT[:, k, :], KT,
                                     (lambda k: s1["h"].after(l, KT + k + 1)) if f == half == 0 else None).then_inc(
                                         full[b], 1)
                        elif kind == "down":
                            n = st[1]
                            if n == 0:
                                pe.sem_inc(held, 1)
                                pe.wait_ge(*bk1.taken(l, ("u", FT1 - 1)))
                            pe.wait_ge(*sl1.ready(l, ("down", n)))
                            w = ring[:, sl1.slot(("down", n)), 0:FT1 * P].rearrange("p (k n) -> p k n", k=FT1)
                            gemm(dst[:, :], lambda k: w[:, k, :], lambda k: U[:, k, :], FT1).then_inc(*done)

            if do2:
                with pe.Fori(0, DEPTH) as layer:
                    l = fresh(pe, layer)
                    for step, st in enumerate(STEPS2):
                        if step % RENEW == RENEW - 1:
                            l = fresh(pe, layer)
                        kind = st[0]
                        jobs = jobs2(st)
                        for job, _ in jobs:
                            pe.wait_ge(*bk2.before(l, job))
                        if kind == "ys":
                            jobs = [(("post", st[1]), SIDE)]
                        if jobs:
                            dst = bank[bk2.bank(jobs[0][0])]
                            done = (full[bk2.bank(jobs[0][0])], 1)
                        if kind == "mm":
                            mod_product(st[1], ma2.after(l, st[1] + 1), bk2.bank(("mod",)), mr2)
                        elif kind == "norm":
                            for k in range(KT):
                                pe.wait_ge(*s2["sq"].after(l, KT * st[1] + k + 1))
                                mm = pe.matmul(dst[:, :], ones, hT[:, k, :], start=(k == 0), stop=(k == KT - 1))
                            mm.then_inc(*done)
                        elif kind == "proj":
                            n = st[1]
                            if n in (4, 5):
                                key, c = ("mix", 0), P * (n - 4)
                                w = ring[:, sl2.slot(key), 0:2048].rearrange("p (k n) -> p k n", k=KT)
                            else:
                                key = {0: ("cq", 0), 6: ("xbc", 0), 10: ("z", 0), 14: ("aqk", 0)}[
                                    max(b for b in (0, 6, 10, 14) if b <= n)]
                                c = P * (n - max(b for b in (0, 6, 10, 14) if b <= n))
                                w = ring[:, sl2.slot(key), :].rearrange("p (k n) -> p k n", k=KT)
                            pe.wait_ge(*sl2.ready(l, key))
                            if n == 3:
                                pe.sem_inc(held, 1)
                                gemm(dst[64:96, :], lambda k: w[:, k, c:c + 32], lambda k: hT[:, k, :],
                                     KT).then_inc(*done)
                            else:
                                gemm(dst[:, :], lambda k: w[:, k, c:c + P], lambda k: hT[:, k, :], KT,
                                     (lambda k: s2["h"].after(l, k + 1)) if n == 0 else None).then_inc(*done)
                        elif kind == "projv":
                            i = st[1]
                            pe.wait_ge(*sl2.ready(l, ("v", 0)))
                            w8 = ring[:, sl2.slot(("v", 0)), :].rearrange("p (k n) -> p k n", k=KT)
                            gemm(dst[:, 0:264], lambda k: hT[:, k, P * i:P * i + P], lambda k: w8[:, k, 0:264],
                                 KT).then_inc(*done)
                        elif kind in ("cqss", "kvss", "an", "sn"):
                            q = [n for n, (job, _) in enumerate(SUMS2) if job == st]
                            w = bd64 if kind == "an" else ones
                            for k in q:
                                pe.wait_ge(*s2["psq"].after(l, k + 1))
                                mm = pe.matmul(dst[:, :], w, sqb[:, k % 2, :], start=(k == q[0]), stop=(k == q[-1]))
                                mm.then_inc(*(done if k == q[-1] else s2["sqr"].up()))
                        elif kind in ("kr", "mqr"):
                            t = KR if kind == "kr" else MQ + st[1]
                            pe.wait_ge(*bk2.taken(l, ("proj", 3) if kind == "kr" else ("mq", st[1])))
                            pe.sem_inc(held, 1)
                            pe.matmul(dst[64:96, :], cst[64:96, C_ROTM + 64:C_ROTM + 96], U[64:96, t, :], start=True,
                                      stop=True).then_inc(*done)
                        elif kind in ("mq", "mk", "mv"):
                            base = ring[:, sl2.slot(("mix", 0)), :]
                            pe.wait_ge(*sl2.ready(l, ("mix", 0)))
                            if kind == "mq":
                                h = st[1]
                                w = base[:, 2048:2816].rearrange("p (k n) -> p k n", k=2)
                                pe.wait_ge(*s2["hn"].after(l, 2))
                                gemm(dst[0:96, :], lambda k: w[:, k, 96 * h:96 * h + 96], lambda k: U[:, CQ + k, :],
                                     2).then_inc(*done)
                            elif kind == "mk":
                                h = st[1]
                                pe.wait_ge(*s2["hn"].after(l, 3))
                                pe.matmul(dst[0:64, :], base[:, 2816 + P * h:2816 + P * h + 64], U[:, CKV, :],
                                          start=True, stop=True).then_inc(*done)
                            else:
                                i = st[1]
                                v = base[:, 2816:3328].rearrange("p (h c) -> p h c", h=4)[:, :, 64:128]
                                pe.wait_ge(*s2["hn"].after(l, 3))
                                pe.matmul(dst[:, 0:256].rearrange("p (h c) -> p h c", h=4),
                                          U[:, CKV, P * i:P * i + P], v, start=True, stop=True).then_inc(*done)
                        elif kind == "dtt":
                            pe.wait_ge(*s2["dt"].after(l, 5))
                            for i in range(QT):
                                mm = pe.transpose(dst[0:8, P * i:P * i + P], dta[:, i, :], ident)
                            mm.then_inc(*done)
                        elif kind == "sc":
                            u = st[1]
                            c, h, i = UNITS2[u]
                            n = P * (i + 1)
                            if u == 0:
                                pe.wait_ge(*bk2.taken(l, ("proj", 17)))
                            if c == "m":
                                pe.wait_ge(*s2["mr"].after(l, 5))
                                pe.sem_inc(held, 1)
                                pe.matmul(dst[:, 0:n], U[0:96, MQ + h, P * i:P * i + P], U[0:96, MK + h, 0:n],
                                          start=True, stop=True).then_inc(*done)
                            else:
                                pe.sem_inc(held, 1)
                                for half in range(2):
                                    b = bk2.bank((("s1", "s2")[half], u))
                                    r = HD * (h % 2) + 32 * half
                                    p = slice(r, r + 32)
                                    pe.matmul(bank[b][:, 0:n], U[p, A_Q + h // 2, P * i:P * i + P],
                                              U[p, A_K + h // 2, 0:n], start=True, stop=True,
                                              tile_position=(r, 0)).then_inc(full[b], 1)
                        elif kind == "tp":
                            u = st[1]
                            pe.wait_ge(*s2["pr"].after(l, u + 1))
                            for j in range(UNITS2[u][2] + 1):
                                mm = pe.transpose(dst[:, P * j:P * j + P], S[:, u % 3, P * j:P * j + P], ident)
                            mm.then_inc(*done)
                        elif kind == "pv":
                            u = st[1]
                            c, h, i = UNITS2[u]
                            pe.wait_ge(*bk2.taken(l, ("tp", u)))
                            p = slice(HD * (h % 2), HD * (h % 2) + HD)
                            v = (W_MV if c == "m" else 0) + HD * h
                            for j in range(i + 1):
                                mm = pe.matmul(dst[p, 0:P], VT[:, j, v:v + HD], pT[:, u % 3, P * j:P * j + P],
                                               start=(j == 0), stop=(j == i))
                            mm.then_inc(*done)
                        elif kind == "xd":
                            pe.wait_ge(*s2["silu"].after(l, 10))
                            for t in range(4):
                                mm = pe.transpose(dst[:, P * t:P * t + P], U[:, XC + t, P * st[1]:P * st[1] + P], ident)
                            mm.then_inc(*done)
                        elif kind == "G":
                            _, g, s = st
                            p = slice(64 * g, 64 * g + 64)
                            pe.matmul(dst[:, P * s:SEQ], U[p, BC, P * s:P * s + P], U[p, CC, P * s:SEQ], start=True,
                                      stop=True).then_inc(*done)
                        elif kind == "da":
                            h = st[1]
                            pe.sem_inc(held, 1)
                            if h == 0:
                                pe.wait_ge(*bk2.taken(l, ("dtt",)))
                                pe.sem_inc(held, 1)
                            pe.matmul(dst[:, :], cst[0:8, C_SELH + P * h:C_SELH + P * h + P], dtf[:, :], start=True,
                                      stop=True).then_inc(*done)
                        elif kind == "y":
                            h = st[1]
                            p = slice(HD * (h % 2), HD * (h % 2) + HD)
                            for s in range(QT):
                                pe.wait_ge(*s2["m"].after(l, 4 * h + s + 1))
                                mm = pe.matmul(dst[p, P * s:SEQ], sel[:, s, HD * h:HD * h + HD],
                                               mixing(4 * h + s)[:, P * s:SEQ], start=(s == 0), stop=(s == QT - 1))
                            mm.then_inc(*done)
                        elif kind == "wo":
                            n = st[1]
                            if n == 0:
                                pe.wait_ge(*s2["hn"].after(l, 9))
                                pe.sem_inc(held, 1)
                                pe.wait_ge(*bk2.taken(l, ("pv", len(UNITS2) - 1)))
                            pe.wait_ge(*sl2.ready(l, ("wo", n // 4)))
                            w8 = ring[:, sl2.slot(("wo", n // 4)), :].rearrange("p (k n) -> p k n", k=KT)
                            c = P * (n % 4)
                            gemm(dst[:, :], lambda k: w8[:, k, c:c + P], lambda k: hT[:, k, :], KT).then_inc(*done)
                        elif kind == "ys":
                            _, w, n = st
                            q = 9 + KT * w + n
                            pe.wait_ge(*s2["psq"].after(l, q + 1))
                            mm = pe.matmul(dst[:, :], ones, sqb[:, q % 2, :], start=(n == 0), stop=(n == KT - 1))
                            mm.then_inc(*(done if n == KT - 1 else s2["sqr"].up()))
                        elif kind == "up":
                            f = st[1]
                            pe.wait_ge(*sl2.ready(l, ("up", f // 4)))
                            w8 = ring[:, sl2.slot(("up", f // 4)), :].rearrange("p (k n) -> p k n", k=KT)
                            c = P * (f % 4)
                            gemm(dst[:, :], lambda k: w8[:, k, c:c + P], lambda k: hT[:, k, :], KT,
                                 (lambda k: s2["h"].after(l, KT + k + 1)) if f == 0 else None).then_inc(*done)
                        elif kind == "down":
                            n = st[1]
                            if n == 0:
                                pe.wait_ge(*s2["u"].after(l, FT2))
                            pe.wait_ge(*sl2.ready(l, ("down", n)))
                            w = ring[:, sl2.slot(("down", n)), :].rearrange("p (k n) -> p k n", k=FT2)
                            gemm(dst[:, :], lambda k: w[:, k, :], lambda k: U[:, k, :], FT2).then_inc(*done)

            if do2:
                pe.wait_ge(*s2["x"].after(DEPTH - 1, 2 * KT))
            else:
                for n in range(KT):
                    pe.wait_ge(*bk1.taken(DEPTH - 1, ("down", n)))
            for i in range(QT):
                for half in range(2):
                    b = 2 * i + half
                    pe.wait_ge(free[b], final[b])
                    for t in range(4):
                        mm = pe.transpose(bank[b][:, P * t:P * t + P], xT[:, 4 * half + t, P * i:P * i + P], ident)
                    mm.then_inc(full[b], 1)

        @block.scalar
        def _(act):
            act.wait_ge(x_in, 48)
            act.wait_ge(cst_in, 16)
            act.preload_act_table_set("natural_log_exp_and_others")
            act.activation(csc[:, :, :], cT[:, :, :], ACT.Exp, scale=-1.0).then_inc(c_exp, 1)
            if do1:
                act.wait_ge(vec_in, 16 * VEC_DMAS1)
                with act.Fori(0, DEPTH) as layer:
                    l = fresh(act, layer)
                    act.preload_act_table_set("natural_log_exp_and_others")
                    act.sem_clear(act_order.sem)
                    act_order.n = 0
                    for step, st in enumerate(STEPS1):
                        if step % RENEW == RENEW - 1:
                            l = fresh(act, layer)
                        kind = st[0]
                        src = bank[bk1.bank(st)] if jobs1(st) and kind not in ("gu", "mm") else None
                        freed = (free[bk1.bank(st)], 1) if src is not None else None
                        if kind == "norm":
                            w = st[1]
                            for k in range(KT):
                                if w == 0:
                                    act.wait_ge(free[k], 1)
                                    act.sem_inc(held, 1)
                                    act.wait_ge(*bk1.taken_before_second(l, ("down", k)))
                                else:
                                    act.wait_ge(*bk1.taken(l, ("wo", k)))
                                    act.wait_ge(*bk1.ready(l, ("wo", KT - 1)))
                                act.activation(hT[:, k, :], xT[:, k, :], ACT.Square).then_inc(*s1["sq"].up())
                            act.wait_ge(*bk1.ready(l, st))
                            act.activation(rb[:, 0, :], src[:, :], ACT.Ln, bias=eps, scale=1.0 / D).then_inc(*freed)
                            act.wait_ge(*bk1.taken(l, st))
                            act.activation(rb[:, 0, :], rb[:, 0, :], ACT.Exp, scale=-0.5).then_inc(*s1["rstd"].up())
                            if w == 0:
                                act.wait_ge(*s1["mod"].after(l, 1))
                            for k in range(KT):
                                act.wait_ge(*s1["xn"].after(l, KT * w + k + 1))
                                act.activation(hT[:, k, :], hT[:, k, :], ACT.Identity,
                                               bias=modT[:, 24 * w + k:24 * w + k + 1],
                                               scale=modA[:, w, k:k + 1]).then_inc(*s1["h"].up())
                        elif kind == "proj":
                            n = st[1]
                            act.wait_ge(*bk1.ready(l, st))
                            if n in NORMED:
                                k = normed_at[n]
                                if k >= 2:
                                    act.wait_ge(*bk1.ready(l, ("pss", NORMED[k - 2])))
                                act.activation(sqb[:, k % 2, :], src[:, :], ACT.Square).then_inc(*s1["psq"].up())
                            act.activation(PT[:, n, :], src[:, :], ACT.Copy,
                                           scale=1.0 / 16 if n == KI else 1.0).then_inc(*freed)
                        elif kind == "projv":
                            act.wait_ge(*bk1.ready(l, st))
                            act.activation(VT[:, st[1], 0:V_N], src[:, 0:V_N], ACT.Copy).then_inc(*freed)
                        elif kind in ("pss", "on"):
                            k = normed_at[st[1]] if kind == "pss" else n_on + st[1]
                            act.wait_ge(*bk1.ready(l, st))
                            if k >= 2:
                                act.wait_ge(*s1["pn"].after(l, k - 1))
                            r = rb[:, k % 2, :]
                            act.activation(nw[:, k % 2, :], src[:, :], ACT.Identity,
                                           bias=cst[:, C_MISC + 5:C_MISC + 6], scale=-0.5 / HD).then_inc(
                                *act_order.up())
                            act.activation(r, src[:, :], ACT.Ln, bias=eps, scale=1.0 / HD).then_inc(*freed)
                            act.wait_ge(*bk1.taken(l, st))
                            act.wait_ge(*act_order.last())
                            act.activation(r, r, ACT.Exp, scale=-0.5).then_inc(*s1["prs"].up())
                        elif kind == "bz":
                            _, h, kt = st
                            act.wait_ge(*bk1.ready(l, st))
                            if h >= 2:
                                act.wait_ge(*bk1.ready(l, ("bpv", h - 2)))
                            act.activation(Z[:, h % 2, kt, P * kt:SEQ], src[:, P * kt:SEQ], ACT.Copy,
                                           scale=HD ** -0.5).then_inc(*freed)
                        elif kind == "bl":
                            _, h, kt = st
                            act.wait_ge(*s1["bu"].after(l, 4 * h + kt + 1))
                            s = SP[:, h % 2, kt, P * kt:SEQ]
                            act.activation(s, s, ACT.Exp).then_inc(*act_order.up())
                            act.wait_ge(*act_order.last())
                            act.activation(s, s, ACT.Ln, bias=ones[:, 0:1]).then_inc(*s1["bl"].up())
                        elif kind == "br":
                            _, h, kt = st
                            act.wait_ge(*s1["bd"].after(l, 4 * h + kt + 1))
                            z = Z[:, h % 2, kt, P * kt:SEQ]
                            act.activation(z, z, ACT.Exp).then_inc(*s1["ba"].up())
                        elif kind == "sc":
                            u = st[1]
                            c, h, i = UNITS1[u]
                            n = P * len(keys_of(UNITS1[u]))
                            act.wait_ge(*s1["sc"].after(l, u + 1))
                            stat = st1[:, u % 3, :]
                            ins = act.activation(S[:, u % 3, 0:n], S[:, u % 3, 0:n], ACT.Exp, bias=stat[:, 1:2],
                                                 accum_out=stat[:, 2:3])
                            if c == "c":
                                ins = act.activation(stat[:, 3:4], vec[:, V_SINK + h:V_SINK + h + 1], ACT.Exp,
                                                     bias=stat[:, 1:2])
                            ins.then_inc(*s1["ex"].up())
                        elif kind == "tp":
                            u = st[1]
                            n = P * len(keys_of(UNITS1[u]))
                            act.wait_ge(*bk1.ready(l, st))
                            if u >= 3:
                                act.wait_ge(*bk1.ready(l, ("pv", u - 3)))
                            act.activation(pT[:, u % 3, 0:n], src[:, 0:n], ACT.Copy).then_inc(*freed)
                        elif kind == "osq":
                            t = st[1]
                            k = n_on + t
                            if t == 0:
                                act.wait_ge(*bk1.taken(l, ("pv", len(UNITS1) - 1)))
                                act.wait_ge(*bk1.ready(l, ("pss", NORMED[-1])))
                            if t >= 2:
                                act.wait_ge(*bk1.ready(l, ("on", t - 2)))
                            act.activation(sqb[:, k % 2, :], hT[:, t, :], ACT.Square).then_inc(*s1["psq"].up())
                        elif kind == "gu":
                            f = st[1]
                            act.wait_ge(*bk1.ready(l, ("g", f)))
                            b = bk1.bank(("g", f))
                            act.activation(U[:, f, :], bank[b][:, :], ACT.Silu).then_inc(free[b], 1)
                            if f == FT1 - 1:
                                act.preload_act_table_set("natural_log_exp_and_others")
            if do2:
                act.wait_ge(vec2_in, 16 * VEC_DMAS2)
                act.wait_ge(pos_ready, 1)
                act.activation(tab[64:96, :, :], tab[64:96, :, :], ACT.Sin).then_inc(pos_ready, 1)
                act.preload_act_table_set("natural_log_exp_and_others")
                if do1:
                    for n in range(KT - len(MAIN), KT):
                        act.wait_ge(*bk1.taken(DEPTH - 1, ("down", n)))
                with act.Fori(0, DEPTH) as layer:
                    l = fresh(act, layer)
                    act.preload_act_table_set("natural_log_exp_and_others")
                    act.sem_clear(act_order.sem)
                    act_order.n = 0

                    def squares(q, src):
                        if q >= 2:
                            job, last = SUMS2[q - 2]
                            if last:
                                act.wait_ge(*bk2.ready(l, job))
                            else:
                                act.wait_ge(*s2["sqr"].after(l, sum(1 for _, e in SUMS2[:q - 1] if not e)))
                        act.activation(sqb[:, q % 2, :], src, ACT.Square).then_inc(*s2["psq"].up())

                    def root(job, r, scale, e, done):
                        act.wait_ge(*bk2.ready(l, job))
                        b = bk2.bank(job)
                        act.activation(rb[:, r, :], bank[b][:, :], ACT.Ln, bias=e, scale=scale).then_inc(free[b], 1)
                        act.wait_ge(*bk2.taken(l, job))
                        act.activation(rb[:, r, :], rb[:, r, :], ACT.Exp, scale=-0.5).then_inc(*done)

                    for step, st in enumerate(STEPS2):
                        if step % RENEW == RENEW - 1:
                            l = fresh(act, layer)
                        kind = st[0]
                        jobs = jobs2(st)
                        if jobs:
                            src = bank[bk2.bank(jobs[0][0])]
                            freed = (free[bk2.bank(jobs[0][0])], 1)
                        if kind == "prep":
                            act.wait_ge(*s2["lam"].after(l, 2))
                            act.activation(sm[:, 2:4], sm[:, 0:2], ACT.Exp).then_inc(*s2["lexp"].up())
                            act.activation(sm[:, 8:16], vec[:, W_ALOG:W_ALOG + 8], ACT.Exp).then_inc(*s2["lexp"].up())
                        elif kind == "norm":
                            w = st[1]
                            for k in range(KT):
                                act.wait_ge(*s2["x"].after(l, KT * (w - 1) + k + 1))
                                if w:
                                    act.wait_ge(*bk2.ready(l, ("wo", KT - 1)))
                                act.activation(hT[:, k, :], xT[:, k, :], ACT.Square).then_inc(*s2["sq"].up())
                            root(st, 0, 1.0 / D, eps, s2["rstd"].up())
                            if w == 0:
                                act.wait_ge(*s2["mod"].after(l, 1))
                            for k in range(KT):
                                act.wait_ge(*s2["xn"].after(l, KT * w + k + 1))
                                act.activation(hT[:, k, :], hT[:, k, :], ACT.Identity,
                                               bias=modT[:, 24 * w + k:24 * w + k + 1],
                                               scale=modA[:, w, k:k + 1]).then_inc(*s2["h"].up())
                        elif kind == "proj":
                            n = st[1]
                            act.wait_ge(*bk2.ready(l, st))
                            if n < 3:
                                squares(n, src[:, :])
                            p = slice(64, 96) if n == 3 else slice(0, P)
                            act.activation(U[p, PROJ2[n], :], src[p, :], ACT.Copy).then_inc(*freed)
                        elif kind == "projv":
                            act.wait_ge(*bk2.ready(l, st))
                            act.activation(VT[:, st[1], 0:264], src[:, 0:264], ACT.Copy).then_inc(*freed)
                        elif kind == "cqss":
                            root(st, 1, 1.0 / 256, eps, s2["prs"].up())
                        elif kind == "kvss":
                            root(st, 0, 1.0 / P, eps, s2["prs"].up())
                        elif kind == "mq":
                            act.wait_ge(*bk2.ready(l, st))
                            act.activation(U[0:96, MQ + st[1], :], src[0:96, :], ACT.Copy).then_inc(*freed)
                        elif kind == "mk":
                            act.wait_ge(*bk2.ready(l, st))
                            act.activation(U[0:64, MK + st[1], :], src[0:64, :], ACT.Copy).then_inc(*freed)
                        elif kind == "mv":
                            act.wait_ge(*bk2.ready(l, st))
                            act.activation(VT[:, st[1], W_MV:W_MV + 256], src[:, 0:256], ACT.Copy).then_inc(*freed)
                        elif kind == "dt":
                            act.wait_ge(*s2["dt"].after(l, 2))
                            act.activation(dtu[:, :, :], dtu[:, :, :], ACT.Exp).then_inc(*act_order.up())
                            act.wait_ge(*act_order.last())
                            act.activation(dtu[:, :, :], dtu[:, :, :], ACT.Ln, bias=ones[:, 0:1]).then_inc(
                                *s2["dt"].up())
                        elif kind == "dtt":
                            act.wait_ge(*bk2.ready(l, st))
                            act.activation(dtf[:, :], src[0:8, :], ACT.Copy).then_inc(*freed)
                        elif kind == "silu":
                            act.wait_ge(*s2["cv"].after(l, 6))
                            for t in range(6):
                                act.activation(U[:, XC + t, :], U[:, XC + t, :], ACT.Silu).then_inc(*s2["silu"].up())
                            for t in range(4):
                                act.wait_ge(*bk2.taken(l, ("proj", 10 + t)))
                                act.activation(U[:, ZT + t, :], U[:, ZT + t, :], ACT.Silu).then_inc(*s2["silu"].up())
                            act.preload_act_table_set("natural_log_exp_and_others")
                        elif kind == "sc":
                            u = st[1]
                            c, h, i = UNITS2[u]
                            n = P * (i + 1)
                            act.wait_ge(*s2["sc"].after(l, u + 1))
                            stat = st1[:, u % 3, :]
                            scale = 32 ** -0.5 if c == "d" else 96 ** -0.5
                            ins = act.activation(S[:, u % 3, 0:n], S[:, u % 3, 0:n], ACT.Exp, bias=stat[:, 2:3],
                                                 scale=scale, accum_out=stat[:, 4:5])
                            if c == "d":
                                ins = act.activation(sel[:, u % 3, 0:n], sel[:, u % 3, 0:n], ACT.Exp,
                                                     bias=stat[:, 3:4], scale=scale, accum_out=stat[:, 5:6])
                            ins.then_inc(*s2["ex"].up())
                        elif kind == "tp":
                            u = st[1]
                            n = P * (UNITS2[u][2] + 1)
                            act.wait_ge(*bk2.ready(l, st))
                            if u >= 3:
                                act.wait_ge(*bk2.ready(l, ("pv", u - 3)))
                            act.activation(pT[:, u % 3, 0:n], src[:, 0:n], ACT.Copy).then_inc(*freed)
                        elif kind == "asq":
                            if st[1] == 0:
                                act.wait_ge(*bk2.taken(l, ("pv", len(UNITS2) - 1)))
                            squares(3 + st[1], hT[:, st[1], :])
                        elif kind == "an":
                            root(st, st[1], 1.0 / HD, cst[:, C_MISC + 1:C_MISC + 2], s2["prs"].up())
                        elif kind == "G":
                            _, g, s = st
                            act.wait_ge(*bk2.ready(l, st))
                            act.activation(U[:, GT[g][s], P * s:SEQ], src[:, P * s:SEQ], ACT.Copy).then_inc(*freed)
                        elif kind == "da":
                            h = st[1]
                            act.wait_ge(*bk2.ready(l, st))
                            if h >= 2:
                                act.wait_ge(*s2["m"].after(l, 4 * (h - 1)))
                            act.activation(tmp[:, h % 2, :], src[:, :], ACT.Exp).then_inc(*freed)
                        elif kind == "sn":
                            g = st[1]
                            for t in range(2):
                                act.wait_ge(*s2["sz"].after(l, 2 * g + t + 1))
                                squares(5 + 2 * g + t, hT[:, 4 + 2 * g + t, :])
                            act.wait_ge(*s2["hn"].after(l, 4 + g))
                            root(st, g, 1.0 / 256, eps, s2["prs"].up())
                        elif kind in ("wo", "down"):
                            n = st[1]
                            w = 0 if kind == "wo" else 1
                            act.wait_ge(*bk2.ready(l, st))
                            squares(9 + KT * w + n, src[:, :])
                            to = U[:, n, :] if w == 0 else hT[:, n, :]
                            act.activation(to, src[:, :], ACT.Copy).then_inc(*freed)
                        elif kind == "post":
                            w = st[1]
                            if w == 0:
                                act.wait_ge(*s2["hn"].after(l, 9))
                            root(st, w, 1.0 / D, eps, s2["rstd"].up())
                        elif kind == "up":
                            f = st[1]
                            act.wait_ge(*bk2.ready(l, st))
                            if f < KT:
                                act.wait_ge(*s2["x"].after(l, KT))
                            act.activation(U[:, f, :], src[:, :], ACT.Relu).then_inc(*freed)

        @block.vector
        def _(dve):
            def link(ins):
                ins.then_inc(*dve_order.up())
                dve.wait_ge(*dve_order.last())

            for t in range(KT):
                dve.wait_ge(full[t], 1)
                dve.tensor_copy(xT[:, t, :], bank[t][:, :]).then_inc(free[t], 1)
            dve.wait_ge(c_exp, 1)
            link(dve.tensor_scalar(csc[:, :, :], csc[:, :, :], 1.0, None, ALU.add))
            link(dve.reciprocal(csc[:, :, :], csc[:, :, :]))
            for l in range(LAYERS):
                link(dve.tensor_tensor(c4[:, l, :], cT[:, l // DEPTH, :], csc[:, l // DEPTH, :], ALU.mult))

            def mod_sum(p, landed_at, read_at, c):
                dve.wait_ge(*landed_at)
                if read_at:
                    dve.wait_ge(*read_at)
                a, w = acc[p % 2], stage[p % 2]
                link(dve.tensor_scalar(a, w[:, 0, :], c[:, 0:1], None, ALU.mult))
                for k in range(1, KT):
                    ins = dve.scalar_tensor_tensor(a, w[:, k, :], c[:, k:k + 1], a, ALU.mult, ALU.add)
                    if k < KT - 1:
                        link(ins)
                ins.then_inc(macc, 1)

            def mod_bias(ready_at, b, bias):
                dve.wait_ge(*ready_at)
                dve.tensor_tensor(modN[:, :], bank[b][:, 0:6 * KT], bias, ALU.add).then_inc(free[b], 1)

            first = 0 if do1 else DEPTH
            for p in range(PIECES):
                mod_sum(p, (mland[p % 2], 16 * (p // 2 + 1)), (mread, p - 1) if p >= 2 else None, c4[:, first, :])
            dve.wait_ge(mod_in, 16 * LAYERS)
            mod_bias((full[0], 2), 0, bias4[:, first, :])
            dve.wait_ge(free[0], 2)
            def normed(l, t, g, k):
                a = tmp[:, 1, :]
                if s1["pn"].seen:
                    dve.wait_ge(*s1["pn"].after(l, s1["pn"].seen))
                link(dve.tensor_tensor(a, rb[:, k % 2, :], rb[:, k % 2, :], ALU.mult))
                link(dve.tensor_tensor(a, a, nw[:, k % 2, :], ALU.mult))
                link(dve.scalar_tensor_tensor(t, t, g, rb[:, k % 2, :], ALU.mult, ALU.mult))
                return dve.scalar_tensor_tensor(t, a, 1.5, t, ALU.add, ALU.mult)

            if do1:
                dve.wait_ge(vec_in, 16 * VEC_DMAS1)
                with dve.Fori(0, DEPTH) as layer:
                    l = fresh(dve, layer)
                    dve.sem_clear(dve_order.sem)
                    dve_order.n = 0
                    link(dve.tensor_copy(vec[:, 0:V1_N], vall1[:, bass.ds(l, 1), :].rearrange("p o v -> p (o v)")))
                    link(dve.tensor_copy(cN[:, :], c4[:, bass.ds(l + 1, 1), :].rearrange("p o v -> p (o v)")))
                    link(dve.tensor_copy(biasN[:, :], bias4[:, bass.ds(l + 1, 1), :].rearrange("p o v -> p (o v)")))
                    for c in (V_QNA, V_QNC):
                        link(dve.tensor_scalar(vec[:, c:c + 1], vec[:, c:c + 1], HD ** -0.5, None, ALU.mult))
                    for step, st in enumerate(STEPS1):
                        if step % RENEW == RENEW - 1:
                            l = fresh(dve, layer)
                        kind = st[0]
                        src = bank[bk1.bank(st)] if jobs1(st) and kind not in ("gu", "mm") else None
                        freed = (free[bk1.bank(st)], 1) if src is not None else None
                        if kind == "prep":
                            link(dve.tensor_copy(modT[:, :], modN[:, :]))
                            for w, g in ((0, V_LN1), (1, V_LN2)):
                                ins = dve.scalar_tensor_tensor(modA[:, w, :], modT[:, 8 + 24 * w:16 + 24 * w], 1.0,
                                                               vec[:, g:g + 8], ALU.add, ALU.mult)
                                if w == 0:
                                    link(ins)
                            ins.then_inc(*s1["mod"].up())
                        elif kind == "ma":
                            p = st[1]
                            mod_sum(p, ml1[p % 2].after(l, 16 * (p // 2 + 1)), mr1.after(l, p - 1) if p >= 2 else None,
                                    cN[:, :])
                        elif kind == "mb":
                            mod_bias(bk1.ready(l, ("mod",)), bk1.bank(("mod",)), biasN[:, :])
                            dve.wait_ge(*bk1.taken(l, ("mod",)))
                        elif kind == "norm":
                            w = st[1]
                            dve.wait_ge(*s1["rstd"].after(l, w + 1))
                            for k in range(KT):
                                dve.tensor_tensor(hT[:, k, :], xT[:, k, :], rb[:, 0, :], ALU.mult).then_inc(
                                    *s1["xn"].up())
                        elif kind == "pss":
                            n = st[1]
                            k = normed_at[n]
                            dve.wait_ge(*s1["prs"].after(l, k + 1))
                            g = {KA: V_KNA, QA: V_QNA, QA + 1: V_QNA, KC: V_KNC, KC + 1: V_KNC}.get(n, V_QNC)
                            normed(l, PT[:, n, :], vec[:, g:g + 1], k).then_inc(*s1["pn"].up())
                        elif kind == "rope":
                            n = st[1]
                            dve.wait_ge(*bk1.ready(l, st))
                            if roped_at[n]:
                                dve.wait_ge(*s1["rope"].after(l, roped_at[n]))
                            dve.tensor_tensor(tmp[:, 0, :], src[:, :], cst[:, C_SIN:C_SIN + SEQ], ALU.mult).then_inc(
                                *freed)
                            link(dve.tensor_tensor(PT[:, n, :], PT[:, n, :], cst[:, C_COS:C_COS + SEQ], ALU.mult))
                            dve.wait_ge(*bk1.taken(l, st))
                            dve.tensor_tensor(PT[:, n, :], PT[:, n, :], tmp[:, 0, :], ALU.add).then_inc(
                                *s1["rope"].up())
                        elif kind == "idx":
                            _, i, h = st
                            n = P * (i + 1)
                            dve.wait_ge(*bk1.ready(l, st))
                            dve.wait_ge(*bk1.taken(l, ("projv", i)))
                            w = VT[:, i, V_WI + h:V_WI + h + 1]
                            to = sel[:, i, 0:n] if h == 0 else tmp[:, 1, 0:n]
                            dve.tensor_scalar(to, src[:, 0:n], 0.0, w, ALU.max, ALU.mult).then_inc(*freed)
                            dve.wait_ge(*bk1.taken(l, st))
                            if h > 0:
                                link(dve.tensor_tensor(sel[:, i, 0:n], sel[:, i, 0:n], tmp[:, 1, 0:n], ALU.add))
                            if h == 3:
                                d = sel[:, i, P * i:P * i + P]
                                link(dve.tensor_tensor(d, d, cst[:, C_CAUSALNEG:C_CAUSALNEG + P], ALU.add))
                        elif kind == "topk":
                            i = st[1]
                            s = sel[:, i, 0:P * (i + 1)]
                            link(dve.max(m8[:, :], s))
                            link(dve.match_replace(s, m8[:, :], s, TAKEN))
                        elif kind == "seldone":
                            s = sel[:, st[1], 0:P * (st[1] + 1)]
                            link(dve.tensor_scalar(s, s, 0.99 * TAKEN, NEG, ALU.is_gt, ALU.mult))
                        elif kind == "bz":
                            _, h, kt = st
                            dve.wait_ge(*bk1.taken(l, st))
                            if h >= 2:
                                for j in range(QT):
                                    dve.wait_ge(*bk1.ready(l, ("br", h - 2, j)))
                            z = Z[:, h % 2, kt, P * kt:SEQ]
                            dve.scalar_tensor_tensor(SP[:, h % 2, kt, P * kt:SEQ], z, -1.0, z, ALU.mult,
                                                     ALU.min).then_inc(*s1["bu"].up())
                        elif kind == "bs":
                            _, h, kt = st
                            dve.wait_ge(*s1["bl"].after(l, 4 * h + kt + 1))
                            s = SP[:, h % 2, kt, P * kt:SEQ]
                            link(dve.scalar_tensor_tensor(s, Z[:, h % 2, kt, P * kt:SEQ], 0.0, s, ALU.max, ALU.add))
                            s = SP[:, h % 2, kt, P * kt:P * kt + P]
                            dve.tensor_tensor(s, s, cst[:, C_STRICT:C_STRICT + P], ALU.mult).then_inc(*s1["bsp"].up())
                        elif kind == "br":
                            _, h, kt = st
                            dve.wait_ge(*bk1.ready(l, st))
                            z = Z[:, h % 2, kt, P * kt:SEQ]
                            dve.tensor_tensor(z, z, src[:, P * kt:SEQ], ALU.subtract).then_inc(*freed)
                            dve.wait_ge(*bk1.taken(l, st))
                            z = Z[:, h % 2, kt, P * kt:P * kt + P]
                            dve.tensor_tensor(z, z, cst[:, C_STRICTNEG:C_STRICTNEG + P], ALU.add).then_inc(
                                *s1["bd"].up())
                        elif kind == "bpv":
                            h = st[1]
                            p = slice(HD * (h % 2), HD * (h % 2) + HD)
                            dve.wait_ge(*bk1.ready(l, st))
                            dve.tensor_copy(hT[p, 2 + h // 2, :], src[p, :]).then_inc(*freed)
                        elif kind == "sc":
                            u = st[1]
                            c, h, i = UNITS1[u]
                            n = P * len(keys_of(UNITS1[u]))
                            if c == "c":
                                mask = cst[:, C_BAND + 2 * P - n:C_BAND + 2 * P]
                            else:
                                mask = sel[:, i, 0:n] if i else cst[:, C_CAUSALNEG:C_CAUSALNEG + P]
                            dve.wait_ge(*bk1.ready(l, st))
                            if u >= 3:
                                dve.wait_ge(*bk1.ready(l, ("tp", u - 3)))
                            dve.sem_inc(held, 1)
                            stat = st1[:, u % 3, :]
                            dve.tensor_tensor_reduce(S[:, u % 3, 0:n], src[:, 0:n], mask, 1.0, 3.0 * NEG, ALU.add,
                                                     ALU.max, stat[:, 0:1]).then_inc(*freed)
                            dve.wait_ge(*bk1.taken(l, st))
                            if c == "c":
                                ins = dve.tensor_scalar(stat[:, 1:2], stat[:, 0:1], vec[:, V_SINK + h:V_SINK + h + 1],
                                                        -1.0, ALU.max, ALU.mult)
                            else:
                                ins = dve.tensor_scalar(stat[:, 1:2], stat[:, 0:1], -1.0, None, ALU.mult)
                            ins.then_inc(*s1["sc"].up())
                        elif kind == "nr":
                            u = st[1]
                            c, h, i = UNITS1[u]
                            n = P * len(keys_of(UNITS1[u]))
                            stat = st1[:, u % 3, :]
                            dve.wait_ge(*s1["ex"].after(l, u + 1))
                            if c == "c":
                                link(dve.tensor_tensor(stat[:, 2:3], stat[:, 2:3], stat[:, 3:4], ALU.add))
                            link(dve.reciprocal(stat[:, 4:5], stat[:, 2:3]))
                            dve.tensor_scalar(S[:, u % 3, 0:n], S[:, u % 3, 0:n], stat[:, 4:5], None,
                                              ALU.mult).then_inc(*s1["pr"].up())
                        elif kind == "pv":
                            c, h, i = UNITS1[st[1]]
                            p = slice(HD * (h % 2), HD * (h % 2) + HD)
                            t = (4 if c == "c" else 0) + h // 2
                            dve.wait_ge(*bk1.ready(l, st))
                            dve.tensor_copy(hT[p, t, P * i:P * i + P], src[p, 0:P]).then_inc(*freed)
                        elif kind == "on":
                            t = st[1]
                            k = n_on + t
                            dve.wait_ge(*s1["prs"].after(l, k + 1))
                            normed(l, hT[:, t, :], vec[:, V_GOUT + t:V_GOUT + t + 1], k).then_inc(*s1["pn"].up())
                        elif kind in ("wo", "down"):
                            n = st[1]
                            g = (16 if kind == "wo" else 40) + n
                            dve.wait_ge(*bk1.ready(l, st))
                            dve.scalar_tensor_tensor(xT[:, n, :], src[:, :], modT[:, g:g + 1], xT[:, n, :], ALU.mult,
                                                     ALU.add).then_inc(*freed)
                        elif kind == "gu":
                            f = st[1]
                            dve.wait_ge(*bk1.ready(l, ("u", f)))
                            dve.wait_ge(*bk1.taken(l, ("g", f)))
                            b = bk1.bank(("u", f))
                            dve.tensor_tensor(U[:, f, :], U[:, f, :], bank[b][:, :], ALU.mult).then_inc(free[b], 1)
            if do2:
                dve.wait_ge(pos_in, 16)
                dve.wait_ge(vec2_in, 16 * VEC_DMAS2)
                rows = slice(64, 96)
                pf, turns, ang = S[rows, 0, :], S[rows, 1, :], S[rows, 2, :]
                if do1:
                    dve.wait_ge(*bk1.ready(DEPTH - 1, ("tp", len(UNITS1) - 1)))
                link(dve.tensor_copy(pf, posi[rows, :]))
                link(dve.tensor_scalar(ang, pf, cst[rows, C_MISC + 4:C_MISC + 5], None, ALU.mult))
                for t, quarter in ((0, 0.25), (1, 0.0)):
                    a = tab[rows, t, :]
                    link(dve.tensor_scalar(turns, ang, 1.0 / TWO_PI, quarter, ALU.mult, ALU.add))
                    link(dve.tensor_scalar(turns, turns, ROUND, None, ALU.add))
                    link(dve.tensor_scalar(turns, turns, ROUND, None, ALU.subtract))
                    link(dve.scalar_tensor_tensor(a, turns, -PI_A, ang, ALU.mult, ALU.add))
                    link(dve.scalar_tensor_tensor(a, turns, -PI_B, a, ALU.mult, ALU.add))
                    link(dve.scalar_tensor_tensor(a, turns, -PI_C, a, ALU.mult, ALU.add))
                    link(dve.tensor_scalar(a, a, quarter * TWO_PI, PI_MAX, ALU.add, ALU.min))
                    ins = dve.tensor_scalar(a, a, -PI_MAX, None, ALU.max)
                    if t == 0:
                        link(ins)
                ins.then_inc(pos_ready, 1)
                dve.wait_ge(pos_ready, 2)
                dve.sem_inc(s2["x"].sem, KT)
                with dve.Fori(0, DEPTH) as layer:
                    l = fresh(dve, layer)
                    dve.sem_clear(dve_order.sem)
                    dve_order.n = 0
                    link(dve.tensor_copy(vec[:, :], vall2[:, bass.ds(l, 1), :].rearrange("p o v -> p (o v)")))
                    for step, st in enumerate(STEPS2):
                        if step % RENEW == RENEW - 1:
                            l = fresh(dve, layer)
                        kind = st[0]
                        jobs = jobs2(st)
                        if jobs:
                            src = bank[bk2.bank(jobs[0][0])]
                            freed = (free[bk2.bank(jobs[0][0])], 1)
                        if kind == "ma":
                            p = st[1]
                            mod_sum(p, ml2[p % 2].after(l, 16 * (p // 2 + 1)), mr2.after(l, p - 1) if p >= 2 else None,
                                    c4[:, LAYERS - 1, :])
                        elif kind == "mb":
                            mod_bias(bk2.ready(l, ("mod",)), bk2.bank(("mod",)), bias4[:, LAYERS - 1, :])
                            dve.wait_ge(*bk2.taken(l, ("mod",)))
                        elif kind == "prep":
                            link(dve.tensor_copy(modT[:, :], modN[:, :]))
                            for w in range(2):
                                link(dve.scalar_tensor_tensor(
                                    modA[:, w, :], modT[:, 8 + 24 * w:16 + 24 * w], 1.0,
                                    vec[:, W_NG + 16 * w:W_NG + 16 * w + 8], ALU.add, ALU.mult))
                                ins = dve.tensor_tensor(modG[:, w, :], modT[:, 16 + 24 * w:24 + 24 * w],
                                                        vec[:, W_NG + 16 * w + 8:W_NG + 16 * w + 16], ALU.mult)
                                if w == 0:
                                    link(ins)
                            ins.then_inc(*s2["mod"].up())
                            for w in range(2):
                                a = vec[:, W_LAM + 64 * w:W_LAM + 64 * w + 32]
                                b = vec[:, W_LAM + 64 * w + 32:W_LAM + 64 * w + 64]
                                link(dve.tensor_tensor(sm[:, 16:48], a, b, ALU.mult))
                                dve.tensor_reduce(sm[:, w:w + 1], sm[:, 16:48], AX.X, ALU.add).then_inc(
                                    *s2["lam"].up())
                                dve.wait_ge(*s2["lam"].after(l, w + 1))
                            dve.wait_ge(*s2["lexp"].after(l, 2))
                            link(dve.tensor_tensor(sm[:, 4:5], sm[:, 3:4], sm[:, 2:3], ALU.subtract))
                            link(dve.tensor_tensor(sm[:, 4:5], sm[:, 4:5], vec[:, W_LI:W_LI + 1], ALU.subtract))
                            link(dve.tensor_scalar(sm[:, 5:6], vec[:, W_LI:W_LI + 1], -1.0, 1.0, ALU.mult, ALU.add))
                            link(dve.tensor_tensor(sm[:, 5:6], sm[:, 5:6], vec[:, W_SUBLN:W_SUBLN + 1], ALU.mult))
                        elif kind == "norm":
                            w = st[1]
                            dve.wait_ge(*s2["rstd"].after(l, 2 * w + 1))
                            for k in range(KT):
                                dve.tensor_tensor(hT[:, k, :], xT[:, k, :], rb[:, 0, :], ALU.mult).then_inc(
                                    *s2["xn"].up())
                        elif kind in ("cqss", "kvss"):
                            tiles, g, r = ((CQ, CQ + 1), W_QN, 1) if kind == "cqss" else ((CKV,), W_KVN, 0)
                            dve.wait_ge(*s2["prs"].after(l, 1 if kind == "cqss" else 2))
                            for k, t in enumerate(tiles):
                                dve.scalar_tensor_tensor(U[:, t, :], U[:, t, :], vec[:, g + k:g + k + 1], rb[:, r, :],
                                                         ALU.mult, ALU.mult).then_inc(*s2["hn"].up())
                        elif kind in ("kr", "mqr"):
                            n = 0 if kind == "kr" else st[1] + 1
                            t = KR if kind == "kr" else MQ + st[1]
                            dve.wait_ge(*bk2.ready(l, st))
                            if n:
                                dve.wait_ge(*s2["mr"].after(l, n))
                            dve.tensor_tensor(tmp[64:96, 0, :], src[64:96, :], tab[64:96, 1, :], ALU.mult).then_inc(
                                *freed)
                            link(dve.tensor_tensor(U[64:96, t, :], U[64:96, t, :], tab[64:96, 0, :], ALU.mult))
                            dve.wait_ge(*bk2.taken(l, st))
                            to = [MK, MK + 1, MK + 2, MK + 3] if kind == "kr" else [t]
                            for k in to:
                                ins = dve.tensor_tensor(U[64:96, k, :], U[64:96, t, :], tmp[64:96, 0, :], ALU.add)
                            ins.then_inc(*s2["mr"].up())
                        elif kind == "dt":
                            for i in range(QT):
                                dve.wait_ge(*bk2.taken(l, ("projv", i)))
                            dve.tensor_tensor(dtt[:, :, :], VT[:, :, W_DT:W_DT + 8],
                                              vec[:, W_DTB:W_DTB + 8].unsqueeze(1).broadcast_to([P, QT, 8]),
                                              ALU.add).then_inc(*s2["dt"].up())
                            dve.wait_ge(*s2["dt"].after(l, 1))
                            dve.scalar_tensor_tensor(dtu[:, :, :], dtt[:, :, :], -1.0, dtt[:, :, :], ALU.mult,
                                                     ALU.min).then_inc(*s2["dt"].up())
                            dve.wait_ge(*s2["dt"].after(l, 3))
                            dve.scalar_tensor_tensor(dtt[:, :, :], dtt[:, :, :], 0.0, dtu[:, :, :], ALU.max,
                                                     ALU.add).then_inc(*s2["dt"].up())
                            dve.wait_ge(*s2["dt"].after(l, 4))
                            link(dve.tensor_scalar(sm[:, 8:16], sm[:, 8:16], -1.0, None, ALU.mult))
                            dve.tensor_tensor(dta[:, :, :], dtt[:, :, :],
                                              sm[:, 8:16].unsqueeze(1).broadcast_to([P, QT, 8]),
                                              ALU.mult).then_inc(*s2["dt"].up())
                        elif kind == "conv":
                            t = st[1]
                            dve.wait_ge(*bk2.taken(l, ("proj", t if t >= 4 else t + 6)))
                            x, a = U[:, XRAW + t, :], U[:, XC + t, :]

                            def tap(j):
                                return vec[:, W_CW + 6 * j + t:W_CW + 6 * j + t + 1]

                            link(dve.tensor_scalar(a, x, tap(3), vec[:, W_CB + t:W_CB + t + 1], ALU.mult, ALU.add))
                            for back in range(1, 4):
                                ins = dve.scalar_tensor_tensor(a[:, back:SEQ], x[:, 0:SEQ - back], tap(3 - back),
                                                               a[:, back:SEQ], ALU.mult, ALU.add)
                                if back < 3:
                                    link(ins)
                            ins.then_inc(*s2["cv"].up())
                        elif kind == "sc":
                            u = st[1]
                            c, h, i = UNITS2[u]
                            n = P * (i + 1)
                            mask = cst[:, C_CHUNK + SEQ - n:C_CHUNK + SEQ]
                            scale = 32 ** -0.5 if c == "d" else 96 ** -0.5
                            if u >= 3:
                                dve.wait_ge(*bk2.ready(l, ("tp", u - 3)))
                            stat = st1[:, u % 3, :]
                            k = 2 if c == "d" else 1
                            for half in range(k):
                                job = (("s1", "s2")[half], u)
                                b = bk2.bank(job)
                                dve.wait_ge(*bk2.ready(l, job))
                                dve.sem_inc(held, 1)
                                to = (S, sel)[half]
                                dve.tensor_tensor_reduce(to[:, u % 3, 0:n], bank[b][:, 0:n], mask, 1.0, 3.0 * NEG,
                                                         ALU.add, ALU.max, stat[:, half:half + 1]).then_inc(free[b], 1)
                                dve.wait_ge(*bk2.taken(l, job))
                            dve.tensor_scalar(stat[:, 2:2 + k], stat[:, 0:k], -scale, None, ALU.mult).then_inc(
                                *s2["sc"].up())
                        elif kind == "nr":
                            u = st[1]
                            c, h, i = UNITS2[u]
                            n = P * (i + 1)
                            stat = st1[:, u % 3, :]
                            dve.wait_ge(*s2["ex"].after(l, u + 1))
                            k = 2 if c == "d" else 1
                            link(dve.reciprocal(stat[:, 6:6 + k], stat[:, 4:4 + k]))
                            s = S[:, u % 3, 0:n]
                            if c == "d":
                                link(dve.tensor_scalar(s, s, stat[:, 6:7], None, ALU.mult))
                                link(dve.tensor_tensor(stat[:, 7:8], stat[:, 7:8], sm[:, 4:5], ALU.mult))
                                dve.scalar_tensor_tensor(s, sel[:, u % 3, 0:n], stat[:, 7:8], s, ALU.mult,
                                                         ALU.add).then_inc(*s2["pr"].up())
                            else:
                                dve.tensor_scalar(s, s, stat[:, 6:7], None, ALU.mult).then_inc(*s2["pr"].up())
                        elif kind == "pv":
                            c, h, i = UNITS2[st[1]]
                            p = slice(HD * (h % 2), HD * (h % 2) + HD)
                            t = (2 if c == "m" else 0) + h // 2
                            dve.wait_ge(*bk2.ready(l, st))
                            dve.tensor_copy(hT[p, t, P * i:P * i + P], src[p, 0:P]).then_inc(*freed)
                        elif kind == "an":
                            t = st[1]
                            dve.wait_ge(*s2["prs"].after(l, 3 + t))
                            dve.scalar_tensor_tensor(hT[:, t, :], hT[:, t, :], sm[:, 5:6], rb[:, t, :], ALU.mult,
                                                     ALU.mult).then_inc(*s2["hn"].up())
                        elif kind == "xd":
                            i = st[1]
                            dve.wait_ge(*bk2.ready(l, st))
                            dve.tensor_tensor(sel[:, i, :].rearrange("p (h d) -> p h d", h=8),
                                              src[:, :].rearrange("p (h d) -> p h d", h=8),
                                              dtt[:, i, :].unsqueeze(2).broadcast_to([P, 8, HD]),
                                              ALU.mult).then_inc(*freed)
                        elif kind == "scan":
                            _, h, s = st
                            m = 4 * h + s
                            dve.wait_ge(*bk2.taken(l, ("da", h)))
                            if m >= 6:
                                dve.wait_ge(*bk2.ready(l, ("y", (m - 6) // 4)))
                            if s == 0 and h % 4 == 0:
                                for j in range(QT):
                                    dve.wait_ge(*bk2.taken(l, ("G", h // 4, j)))
                            x = mixing(m)[:, P * s:SEQ]
                            dve.sem_inc(held, 1)
                            link(dve.tensor_tensor_scan(x, tmp[:, h % 2, P * s:SEQ],
                                                        cst[:, C_DELTA:C_DELTA + SEQ - P * s], 0.0, ALU.mult, ALU.add))
                            dve.tensor_tensor(x, x, U[:, GT[h // 4][s], P * s:SEQ], ALU.mult).then_inc(*s2["m"].up())
                        elif kind == "yo":
                            h = st[1]
                            p = slice(HD * (h % 2), HD * (h % 2) + HD)
                            b = bk2.bank(("y", h))
                            dve.wait_ge(*bk2.ready(l, ("y", h)))
                            dve.scalar_tensor_tensor(hT[p, 4 + h // 2, :], U[p, XC + h // 2, :],
                                                     vec[p, W_DSK + h // 2:W_DSK + h // 2 + 1], bank[b][p, :],
                                                     ALU.mult, ALU.add).then_inc(free[b], 1)
                        elif kind == "sz":
                            for h in range(4, 8):
                                dve.wait_ge(*bk2.taken(l, ("y", h)))
                            for t in range(4):
                                dve.tensor_tensor(hT[:, 4 + t, :], hT[:, 4 + t, :], U[:, ZT + t, :],
                                                  ALU.mult).then_inc(*s2["sz"].up())
                        elif kind == "sn":
                            g = st[1]
                            dve.wait_ge(*s2["prs"].after(l, 5 + g))
                            for t in (2 * g, 2 * g + 1):
                                dve.scalar_tensor_tensor(hT[:, 4 + t, :], hT[:, 4 + t, :],
                                                         vec[:, W_SNG + t:W_SNG + t + 1], rb[:, g, :], ALU.mult,
                                                         ALU.mult).then_inc(*s2["hn"].up())
                        elif kind == "post":
                            w = st[1]
                            dve.wait_ge(*s2["rstd"].after(l, 2 * w + 2))
                            y = U if w == 0 else hT
                            for n in range(KT):
                                link(dve.scalar_tensor_tensor(y[:, n, :], y[:, n, :], modG[:, w, n:n + 1],
                                                              rb[:, w, :], ALU.mult, ALU.mult))
                                dve.tensor_tensor(xT[:, n, :], xT[:, n, :], y[:, n, :], ALU.add).then_inc(
                                    *s2["x"].up())
                        elif kind == "up":
                            f = st[1]
                            dve.wait_ge(*bk2.taken(l, st))
                            dve.tensor_tensor(U[:, f, :], U[:, f, :], U[:, f, :], ALU.mult).then_inc(*s2["u"].up())
            for i in range(QT):
                for half in range(2):
                    b = 2 * i + half
                    dve.wait_ge(full[b], final[b] + 1)
                    ins = dve.tensor_copy(U[:, b, :], bank[b][:, :])
                ins.then_inc(out_ready, 1)

        for s in ([mr1] if do1 else []) + ([mr2] if do2 else []):
            s.check()
        for s in [*(s1.values() if do1 else ()), *(s2.values() if do2 else ())]:
            s.check()


INPUTS = ["x", "c", "ln1", "ln2", "b_mod", "w_in", "qn_a", "kn_a", "qn_c", "kn_c", "sinks", "g_out", "w_o",
          "w_gate", "w_up", "w_down", "c_2",
          "positions_2", "b_ada_2", "norm_g_2", "w_in_2", "diff_lambda_2", "diff_subln_g_2", "mla_q_norm_g_2",
          "w_uq_2", "mla_kv_norm_g_2", "w_ukv_2", "conv_w_2", "conv_b_2", "dt_bias_2", "a_log_2", "d_skip_2",
          "ssm_norm_g_2", "w_out_2", "w_up_2", "w_down_2"]


def kernel(**inputs):
    import concourse.bacc as bacc
    from concourse.bass_utils import run_bass_kernel_spmd

    nc = bacc.Bacc("TRN2", target_bir_lowering=False, num_devices=1)
    arrays, A = {}, {}
    for name in INPUTS:
        a = np.ascontiguousarray(inputs[name])
        arrays["in_" + name] = a
        A[name] = nc.dram_tensor("in_" + name, a.shape, mybir.dt.from_np(a.dtype), kind="ExternalInput").ap()
    mods = np.concatenate([np.asarray(inputs["w_mod"]), np.asarray(inputs["w_ada_2"])])
    arrays["in_w_mods"] = mods
    A["w_mods"] = nc.dram_tensor("in_w_mods", mods.shape, F32, kind="ExternalInput").ap()
    arrays["in_consts"] = constants()
    A["consts"] = nc.dram_tensor("in_consts", (P, C_N), F32, kind="ExternalInput").ap()
    out = nc.dram_tensor("out_x", (1, SEQ, D), F32, kind="ExternalOutput").ap()
    build(nc, A, out, BLOCKS)
    return run_bass_kernel_spmd(nc, [arrays], core_ids=[0]).results[0]["out_x"]


BLOCKS = (1, 2)
```
